# Optimizing a Trainium2 kernel written in Bass

```python
import math
import jax, jax.numpy as jnp
from jax import lax
import numpy as np

D_MODEL = 1024
BATCH = 1
SEQ = 512
DEPTH = 1
DEC_BATCH = 8
DEC_SEQ = 8
PAST_LEN = 4096
PAGE_SIZE = 128

D_LRU = D_MODEL // 2
D_RET = D_MODEL - D_LRU
N_LRU_BLOCKS = 8
LRU_BLOCK = D_LRU // N_LRU_BLOCKS
CONV_W = 4
LRU_C = 8.0
N_RET_HEADS = 4
RET_DK = D_RET // N_RET_HEADS
RET_DV = D_RET // N_RET_HEADS
D_QK = N_RET_HEADS * RET_DK
RET_CHUNK = 128
ROPE_BASE = 10000.0
D_IN_PROJ = 2 * D_LRU + 2 * D_QK + 2 * D_RET
SPLITS = (D_LRU, 2 * D_LRU, 2 * D_LRU + D_QK, 2 * D_LRU + 2 * D_QK, 2 * D_LRU + 2 * D_QK + D_RET)
N_EXPERT_GROUPS = 4
EXPERTS_PER_GROUP = 4
N_EXPERTS = N_EXPERT_GROUPS * EXPERTS_PER_GROUP
TOP_K_IN_GROUP = 2
D_EXPERT = 256
NORM_EPS = 1e-6
GN_EPS = 1e-5

kernel_name = 'hymba_rglru_retention_hmoe_step'

F32 = jnp.float32

def _rmsnorm(x, w):
    xf = x.astype(F32)
    return xf * lax.rsqrt(jnp.mean(xf * xf, axis=-1, keepdims=True) + NORM_EPS) * w.astype(F32)

def _causal_conv(x, buf, w, b):
    t = x.shape[1]
    xx = jnp.concatenate([buf.astype(F32), x], axis=1)
    out = b.astype(F32)
    for j in range(CONV_W):
        out = out + xx[:, j:j + t] * w[j]
    return out, xx[:, t:]

def _rglru(x, h0, w_r, b_r, w_i, b_i, lam):
    bsz, t, _ = x.shape
    xb = x.reshape(bsz, t, N_LRU_BLOCKS, LRU_BLOCK)
    r = jax.nn.sigmoid(jnp.einsum('btnj,njk->btnk', xb, w_r) + b_r).reshape(bsz, t, D_LRU)
    i = jax.nn.sigmoid(jnp.einsum('btnj,njk->btnk', xb, w_i) + b_i).reshape(bsz, t, D_LRU)
    log_a = -LRU_C * r * jax.nn.softplus(-lam.astype(F32))
    a = jnp.exp(log_a)
    u = jnp.sqrt(-jnp.expm1(2.0 * log_a)) * (i * x)

    def step(h, inp):
        a_t, u_t = inp
        h = a_t * h + u_t
        return h, h

    h_last, hs = lax.scan(step, h0.astype(F32), (a.transpose(1, 0, 2), u.transpose(1, 0, 2)))
    return hs.transpose(1, 0, 2), h_last

def _rotary(x, pos):
    half = x.shape[-1] // 2
    inv = ROPE_BASE ** (-jnp.arange(half, dtype=F32) / half)
    ang = pos[:, None] * inv[None, :]
    cos = jnp.cos(ang)[None, :, None, :]
    sin = jnp.sin(ang)[None, :, None, :]
    x1, x2 = x[..., :half], x[..., half:]
    return jnp.concatenate([x1 * cos - x2 * sin, x1 * sin + x2 * cos], axis=-1)

def _retention(q, k, v, s0):
    bsz, t, h, dk = q.shape
    dv = v.shape[-1]
    c = math.gcd(t, RET_CHUNK)
    nc = t // c
    log_g = jnp.log1p(-jnp.exp2(-5.0 - jnp.arange(h, dtype=F32)))
    q = q.reshape(bsz, nc, c, h, dk)
    k = k.reshape(bsz, nc, c, h, dk)
    v = v.reshape(bsz, nc, c, h, dv)
    idx = jnp.arange(c, dtype=F32)
    diff = idx[:, None] - idx[None, :]
    mask = jnp.where(diff[None] >= 0, jnp.exp(jnp.maximum(diff, 0.0)[None] * log_g[:, None, None]), 0.0)
    scores = jnp.einsum('bnihd,bnjhd->bnhij', q, k) * mask[None, None]
    inner = jnp.einsum('bnhij,bnjhe->bnihe', scores, v)
    w_state = jnp.exp((c - 1.0 - idx)[None, :] * log_g[:, None])
    kv = jnp.einsum('bnjhd,hj,bnjhe->nbhde', k, w_state, v)
    chunk_decay = jnp.exp(c * log_g)[:, None, None]

    def step(s, kv_n):
        return chunk_decay * s + kv_n, s

    s_last, s_prev = lax.scan(step, s0.astype(F32), kv)
    cross_decay = jnp.exp((idx + 1.0)[:, None] * log_g[None, :])
    cross = jnp.einsum('bnihd,nbhde->bnihe', q, s_prev) * cross_decay[None, None, :, :, None]
    return (inner + cross).reshape(bsz, t, h, dv), s_last

def _mixer(u, conv_buf, h0, s0, pos, w_in, conv_w, conv_b, w_rgate, b_rgate, w_igate, b_igate,
           lru_lambda, ret_gn_w, w_out):
    bsz, t, _ = u.shape
    z = u @ w_in
    xr, yg, q, k, v, g = jnp.split(z, SPLITS, axis=-1)
    xc, new_buf = _causal_conv(xr, conv_buf, conv_w, conv_b)
    hseq, h_last = _rglru(xc, h0, w_rgate, b_rgate, w_igate, b_igate, lru_lambda)
    out_a = hseq * jax.nn.gelu(yg, approximate=True)
    q = _rotary(q.reshape(bsz, t, N_RET_HEADS, RET_DK), pos) * (RET_DK ** -0.5)
    k = _rotary(k.reshape(bsz, t, N_RET_HEADS, RET_DK), pos)
    v = v.reshape(bsz, t, N_RET_HEADS, RET_DV)
    o, s_last = _retention(q, k, v, s0)
    mu = jnp.mean(o, axis=-1, keepdims=True)
    var = jnp.mean(jnp.square(o - mu), axis=-1, keepdims=True)
    o = ((o - mu) * lax.rsqrt(var + GN_EPS)).reshape(bsz, t, D_RET)
    out_b = o * ret_gn_w * jax.nn.silu(g)
    y = jnp.concatenate([out_a, out_b], axis=-1) @ w_out
    return y, new_buf, h_last, s_last

def _moe(u, w_rg, b_rg, w_re, b_re, w_g, w_u, w_d):
    bsz, t, d = u.shape
    xf = u.reshape(bsz * t, d)
    p_group = jax.nn.softmax((xf @ w_rg + b_rg).astype(F32), axis=-1)
    g_sel = jnp.argmax(p_group, axis=-1)
    p_g = jnp.take_along_axis(p_group, g_sel[:, None], axis=-1)[:, 0]
    e_logits = (xf @ w_re + b_re).astype(F32).reshape(-1, N_EXPERT_GROUPS, EXPERTS_PER_GROUP)
    in_group = jnp.take_along_axis(e_logits, g_sel[:, None, None], axis=1)[:, 0]
    p_e = jax.nn.softmax(in_group, axis=-1)
    top_w, top_i = lax.top_k(p_e, TOP_K_IN_GROUP)
    top_w = top_w / jnp.sum(top_w, axis=-1, keepdims=True)
    expert_id = g_sel[:, None] * EXPERTS_PER_GROUP + top_i
    gates = jnp.sum(jax.nn.one_hot(expert_id, N_EXPERTS, dtype=F32)
                    * (p_g[:, None] * top_w)[..., None], axis=1)
    h = jax.nn.silu(jnp.einsum('nd,edf->nef', xf, w_g)) * jnp.einsum('nd,edf->nef', xf, w_u)
    out = jnp.einsum('nef,efd->nd', h * gates[..., None], w_d)
    return out.reshape(bsz, t, d)

def _layer(x, c, conv_buf, h0, s0, pos, w_mod, b_mod, n_pre1, n_post1, n_pre2, n_post2,
           w_in, conv_w, conv_b, w_rgate, b_rgate, w_igate, b_igate, lru_lambda, ret_gn_w, w_out,
           w_rg, b_rg, w_re, b_re, w_g, w_u, w_d):
    mod = jax.nn.silu(c.astype(F32)) @ w_mod + b_mod
    sh1, sc1, g1, sh2, sc2, g2 = jnp.split(mod, 6, axis=-1)
    u = _rmsnorm(x, n_pre1) * (1.0 + sc1[:, None]) + sh1[:, None]
    m, buf, h_last, s_last = _mixer(u, conv_buf, h0, s0, pos, w_in, conv_w, conv_b, w_rgate, b_rgate,
                                    w_igate, b_igate, lru_lambda, ret_gn_w, w_out)
    x = x + g1[:, None] * _rmsnorm(m, n_post1)
    u2 = _rmsnorm(x, n_pre2) * (1.0 + sc2[:, None]) + sh2[:, None]
    f = _moe(u2, w_rg, b_rg, w_re, b_re, w_g, w_u, w_d)
    x = x + g2[:, None] * _rmsnorm(f, n_post2)
    return x, buf, h_last, s_last

def setup_inputs(seed: int = 0) -> dict:
    key = jax.random.key(seed)
    ks = jax.random.split(key, 32)
    L = DEPTH

    def nrm(k, shape, scale):
        return jax.random.normal(k, shape, F32) * scale

    u_lam = jax.random.uniform(ks[14], (L, D_LRU), F32, 0.9, 0.999)
    p_lam = u_lam ** (1.0 / LRU_C)
    return {
        'x_prompt': nrm(ks[0], (BATCH, SEQ, D_MODEL), 1.0),
        'x_sample': nrm(ks[1], (DEC_BATCH, DEC_SEQ, D_MODEL), 1.0),
        'state_conv': nrm(ks[2], (L, DEC_BATCH, CONV_W - 1, D_LRU), 1.0),
        'state_lru': nrm(ks[3], (L, DEC_BATCH, D_LRU), 0.5),
        'state_ret': nrm(ks[4], (L, DEC_BATCH, N_RET_HEADS, RET_DK, RET_DV), 4.0),
        'c_prompt': nrm(ks[5], (BATCH, D_MODEL), 1.0),
        'c_sample': nrm(ks[6], (DEC_BATCH, D_MODEL), 1.0),
        'w_mod': nrm(ks[7], (L, D_MODEL, 6 * D_MODEL), 0.5 * D_MODEL ** -0.5),
        'b_mod': nrm(ks[8], (L, 6 * D_MODEL), 0.02),
        'norm_pre_mix': 1.0 + nrm(ks[9], (L, D_MODEL), 0.05),
        'norm_post_mix': 1.0 + nrm(ks[10], (L, D_MODEL), 0.05),
        'norm_pre_ffn': 1.0 + nrm(ks[11], (L, D_MODEL), 0.05),
        'norm_post_ffn': 1.0 + nrm(ks[12], (L, D_MODEL), 0.05),
        'w_in': nrm(ks[13], (L, D_MODEL, D_IN_PROJ), D_MODEL ** -0.5),
        'conv_w': nrm(ks[15], (L, CONV_W, D_LRU), CONV_W ** -0.5),
        'conv_b': nrm(ks[16], (L, D_LRU), 0.02),
        'w_rgate': nrm(ks[17], (L, N_LRU_BLOCKS, LRU_BLOCK, LRU_BLOCK), LRU_BLOCK ** -0.5),
        'b_rgate': nrm(ks[18], (L, N_LRU_BLOCKS, LRU_BLOCK), 0.02),
        'w_igate': nrm(ks[19], (L, N_LRU_BLOCKS, LRU_BLOCK, LRU_BLOCK), LRU_BLOCK ** -0.5),
        'b_igate': nrm(ks[20], (L, N_LRU_BLOCKS, LRU_BLOCK), 0.02),
        'lru_lambda': jnp.log(p_lam) - jnp.log1p(-p_lam),
        'ret_gn_w': 1.0 + nrm(ks[21], (L, D_RET), 0.05),
        'w_out': nrm(ks[22], (L, D_MODEL, D_MODEL), D_MODEL ** -0.5),
        'w_router_group': nrm(ks[23], (L, D_MODEL, N_EXPERT_GROUPS), D_MODEL ** -0.5),
        'b_router_group': nrm(ks[24], (L, N_EXPERT_GROUPS), 0.01),
        'w_router_expert': nrm(ks[25], (L, D_MODEL, N_EXPERTS), D_MODEL ** -0.5),
        'b_router_expert': nrm(ks[26], (L, N_EXPERTS), 0.01),
        'w_exp_gate': nrm(ks[27], (L, N_EXPERTS, D_MODEL, D_EXPERT), D_MODEL ** -0.5),
        'w_exp_up': nrm(ks[28], (L, N_EXPERTS, D_MODEL, D_EXPERT), D_MODEL ** -0.5),
        'w_exp_down': nrm(ks[29], (L, N_EXPERTS, D_EXPERT, D_MODEL), D_EXPERT ** -0.5),
    }

def reference(x_prompt, x_sample, state_conv, state_lru, state_ret, c_prompt, c_sample,
              w_mod, b_mod, norm_pre_mix, norm_post_mix, norm_pre_ffn, norm_post_ffn,
              w_in, conv_w, conv_b, w_rgate, b_rgate, w_igate, b_igate, lru_lambda, ret_gn_w, w_out,
              w_router_group, b_router_group, w_router_expert, b_router_expert,
              w_exp_gate, w_exp_up, w_exp_down):
    bp, tp, _ = x_prompt.shape
    bs, ts, _ = x_sample.shape
    pos_p = jnp.arange(tp, dtype=F32)
    pos_s = jnp.float32(PAST_LEN) + jnp.arange(ts, dtype=F32)
    yp = x_prompt.astype(F32)
    ys = x_sample.astype(F32)
    zero_conv = jnp.zeros((bp, CONV_W - 1, D_LRU), F32)
    zero_h = jnp.zeros((bp, D_LRU), F32)
    zero_s = jnp.zeros((bp, N_RET_HEADS, RET_DK, RET_DV), F32)
    conv_p, lru_p, ret_p, conv_s, lru_s, ret_s = [], [], [], [], [], []
    for l in range(DEPTH):
        lw = (w_mod[l], b_mod[l], norm_pre_mix[l], norm_post_mix[l], norm_pre_ffn[l], norm_post_ffn[l],
              w_in[l], conv_w[l], conv_b[l], w_rgate[l], b_rgate[l], w_igate[l], b_igate[l],
              lru_lambda[l], ret_gn_w[l], w_out[l], w_router_group[l], b_router_group[l],
              w_router_expert[l], b_router_expert[l], w_exp_gate[l], w_exp_up[l], w_exp_down[l])
        yp, cb, hb, sb = _layer(yp, c_prompt, zero_conv, zero_h, zero_s, pos_p, *lw)
        conv_p.append(cb); lru_p.append(hb); ret_p.append(sb)
        ys, cb, hb, sb = _layer(ys, c_sample, state_conv[l], state_lru[l], state_ret[l], pos_s, *lw)
        conv_s.append(cb); lru_s.append(hb); ret_s.append(sb)
    return (yp.astype(x_prompt.dtype), ys.astype(x_sample.dtype),
            jnp.stack(conv_p).astype(state_conv.dtype), jnp.stack(lru_p).astype(state_lru.dtype),
            jnp.stack(ret_p).astype(state_ret.dtype),
            jnp.stack(conv_s).astype(state_conv.dtype), jnp.stack(lru_s).astype(state_lru.dtype),
            jnp.stack(ret_s).astype(state_ret.dtype))


_drawn_inputs = setup_inputs


def setup_inputs(seed=0):
    import zlib

    import numpy as np

    out = dict(_drawn_inputs(seed))
    spreads = {}
    factors = {'norm_post_ffn': 4.101,
     'b_rgate': 8.0,
     'b_igate': 2.766,
     'b_router_group': 3.259,
     'b_router_expert': 5.131}
    for name, (base, spread) in spreads.items():
        noise = np.random.default_rng([zlib.crc32(name.encode()), seed]).standard_normal(out[name].shape)
        drawn = base * np.exp(spread * noise) if base else spread * noise
        out[name] = __import__('jax').numpy.asarray(drawn.astype(out[name].dtype))
    for name, factor in factors.items():
        out[name] = (out[name] * factor).astype(out[name].dtype)
    return out
```

```python
import math
from contextlib import ExitStack

import numpy as np

import concourse.bass as bass
from concourse import mybir

ALU = mybir.AluOpType
ACT = mybir.ActivationFunctionType
AX = mybir.AxisListType
F32 = mybir.dt.float32

P = 128
D = 1024
SEQ = 512
DB, DT = 8, 8
NS = DB * DT
NTOK = SEQ + NS
KT = D // P
DL = 512
MT = DL // P
CONVW = 4
NH = 4
DK = 128
PAST = 4096
NE = 16
NG = 4
EPG = 4
FE = 256
FT = FE // P
NORM_EPS = 1e-6
GN_EPS = 1e-5
TILES = SEQ // P + 1
SROWS = NS
XRW = 3 + SEQ + DB * (3 + DT)
NMOD = 3
SLOTS = 9
SLOT = 2048

LOG_G = [math.log1p(-(2.0 ** (-5.0 - h))) for h in range(NH)]
GAMMA_CHUNK = [math.exp(P * g) for g in LOG_G]
GAMMA_STEP = [math.exp(DT * g) for g in LOG_G]

C_ID = 0
C_MP = C_ID + P
C_MS = C_MP + P
C_COS = C_MS + NS
C_SIN = C_COS + TILES * 64
C_DQ = C_SIN + TILES * 64
C_DK = C_DQ + 2 * NH
C_BM = C_DK + 2 * NH
C_REV = C_BM + DB
NCONST = C_REV + NG


def shape_constants():
    c = np.zeros((P, NCONST), np.float32)
    i = np.arange(P)
    c[:, C_ID:C_ID + P] = np.eye(P)
    c[:, C_MP:C_MP + P] = i[:, None] <= i[None, :]
    s = np.arange(NS)
    same = (s[:, None] // DT) == (s[None, :] // DT)
    c[:NS, C_MS:C_MS + NS] = same & (s[:, None] <= s[None, :])
    half = DK // 2
    inv = np.float32(10000.0) ** (-np.arange(half, dtype=np.float32) / np.float32(half))
    for t in range(TILES):
        pos = (t * P + i if t < TILES - 1 else PAST + i % DT).astype(np.float32)
        ang = (pos[:, None] * inv[None, :].astype(np.float32)).astype(np.float32)
        c[:, C_COS + t * 64:C_COS + (t + 1) * 64] = np.cos(ang.astype(np.float64))
        c[:, C_SIN + t * 64:C_SIN + (t + 1) * 64] = np.sin(ang.astype(np.float64))
    for h in range(NH):
        c[:, C_DQ + h] = np.exp((i + 1) * LOG_G[h]) * DK ** -0.5
        c[:, C_DQ + NH + h] = np.exp((i % DT + 1) * LOG_G[h]) * DK ** -0.5
        c[:, C_DK + h] = np.exp(-(i + 1) * LOG_G[h])
        c[:, C_DK + NH + h] = np.exp(-(i % DT + 1) * LOG_G[h])
    for b in range(DB):
        c[b * DT:(b + 1) * DT, C_BM + b] = 1.0
    c[:, C_REV:C_REV + NG] = NG - np.arange(NG)
    return c


def rows(t):
    return P if t < TILES - 1 else SROWS


def weight_pieces():
    out = [("mod", 0, k) for k in range(KT)]
    out += [("in", 0, 0), ("in", 0, 1)] + [("mod", 1, k) for k in range(KT)]
    out += [("in", 1, 0), ("in", 1, 1)] + [("mod", 2, k) for k in range(KT)]
    out += [("in", c, h) for c in range(2, 6) for h in range(2)]
    out += [("out", n, h) for n in range(2) for h in range(2)]
    for e in range(NE):
        out += [("wg", e, 0), ("wu", e, 0), ("wd", e, 0)]
    return out


def used_up(piece):
    kind, a, b = piece
    if kind == "mod":
        return {0: 0, 1: 10, 2: 30}[a] + b
    if kind == "in":
        return {0: 15.5, 1: 35.5}.get(a, 50 + a)
    if kind == "out":
        return 60
    return 70 + a + (0.5 if kind == "wd" else 0)


def place_pieces():
    held = [(-1 + s * 0.01, None) for s in range(SLOTS)]
    uses = [0] * SLOTS
    slot, before, nth = {}, {}, {}
    for p in weight_pieces():
        s = min(range(SLOTS), key=lambda j: held[j][0])
        slot[p], before[p] = s, held[s][1]
        uses[s] += 1
        nth[p] = uses[s]
        held[s] = (used_up(p), p)
    return slot, before, nth


def build(nc, x_prompt, x_sample, state_conv, state_lru, state_ret, c_prompt, c_sample, w_mod, b_mod,
          norm_pre_mix, norm_post_mix, norm_pre_ffn, norm_post_ffn, w_in, conv_w, conv_b, w_rgate,
          b_rgate, w_igate, b_igate, lru_lambda, ret_gn_w, w_out, w_router_group, b_router_group,
          w_router_expert, b_router_expert, w_exp_gate, w_exp_up, w_exp_down, consts,
          y_prompt, y_sample, conv_prompt, lru_prompt, ret_prompt, conv_sample, lru_sample,
          ret_sample):
    slot, before, nth = place_pieces()
    with ExitStack() as ctx:
        def sb(name, shape):
            return ctx.enter_context(nc.sbuf_tensor(name, shape, F32))

        def sem(name):
            return ctx.enter_context(nc.semaphore(name))

        mod_rows_dram = nc.dram_tensor("mod_rows_dram", (1 + DB, 6 * D), F32, kind="Internal").ap()

        bank = [ctx.enter_context(nc.psum_tensor(f"bank{i}", [P, 512], F32)) for i in range(8)]

        x = sb("x", [P, TILES, D])
        uT = sb("uT", [P, KT, NTOK])
        ring = sb("ring", [P, SLOTS, SLOT])
        hy = sb("hy", [P, MT, NTOK])
        outbT = sb("outbT", [P, NH, NTOK])
        rowsT = sb("rowsT", [P, 416])
        con = sb("con", [P, NCONST])
        modT = sb("modT", [P, 4, 4, 32])
        wgate = sb("wgate", [P, 2, MT, 64])
        gnw = sb("gnw", [P, DL])
        wrt = sb("wrt", [P, KT, NG + NE])
        brt = sb("brt", [P, NG + NE])
        ss = sb("ss", [P, 4, TILES, 2])
        softp = sb("softp", [P, 8, MT])
        gst = sb("gst", [P, NH, 6])
        gmv = sb("gmv", [P, NH, 2])
        grs = sb("grs", [P, NH])
        tails = sb("tails", [P, MT, 36])
        logit = sb("logit", [P, TILES, NG + NE])
        gates = sb("gates", [P, TILES, NE])
        tailrow = sb("tailrow", [36, DL])
        rtb = sb("rtb", [P, 168])
        eps = sb("eps", [P, 2])
        arena = sb("arena", [P, 14336])

        def region(at, *dims):
            v = arena[:, at:at + int(np.prod(dims))]
            if len(dims) == 2:
                v = v.rearrange("p (a b) -> p a b", b=dims[1])
            return v

        xn = region(0, TILES, D)
        bm = region(5120, NMOD, 512)
        nm = region(6656, NMOD, 512)
        crow = hy[0:32, 0:2, :].rearrange("p a b -> p (a b)")[:, 0:D]
        par = hy[0:8, 2, 0:DL]
        srow = hy[0:32, 3, 0:DL]
        xr = [region(8192 + i * XRW, XRW) for i in range(2)]
        xc = [region(9408 + i * NTOK, NTOK) for i in range(2)]
        ge = [region(10560 + i * NTOK, NTOK) for i in range(2)]
        R, I, Q = (region(11712 + i * NTOK, NTOK) for i in range(3))
        A = region(13440, NTOK)
        Z = ge[1]
        qs, ks, tB, tS, kr1, vv1, gg1, kr0, vv0, gg0, qr, S, qT, kT, sm, ob = (
            region(i * 512, 512) for i in range(16))
        kr, vv, gg = [kr0, kr1], [vv0, vv1], [gg0, gg1]
        s0 = [region(0, DB, DK), region(1024, DB, DK)]
        vblk = region(2048, DB, DK)
        tab = {n: region(8192 + i * D, D)
               for i, n in enumerate(("g1p", "g1s", "a2p", "a2s", "s2p", "s2s"))}
        tab["g2p"], tab["g2s"] = tab["a2p"], tab["a2s"]
        t1 = region(3072, D)
        u2 = [region(4096, D), region(5120, D)]
        junk = region(6144, D)
        Y = region(0, TILES, D)
        hb = [region(5120 + i * FE, FE) for i in range(2)]
        hg = [region(5632 + i * FE, FE) for i in range(2)]
        hT = [region(6144 + i * FE, FE) for i in range(2)]
        yj = region(6656, D)

        gx = rtb[:, 0:25].rearrange("p (t g) -> p t g", g=5)
        rtop, rtmp, rm1, rm2 = (rtb[:, 25 + 5 * i:30 + 5 * i] for i in range(4))
        rgrp, rsel, rin, rin2, roh1, roh2 = (
            rtb[:, 48 + 20 * i:68 + 20 * i].rearrange("p (t g) -> p t g", g=NG) for i in range(6))

        ident = con[:, C_ID:C_ID + P]
        cosv = con[:, C_COS:C_COS + TILES * 64].rearrange("p (t d) -> p t d", d=64)
        sinv = con[:, C_SIN:C_SIN + TILES * 64].rearrange("p (t d) -> p t d", d=64)
        cT = rowsT[:, 0:256].rearrange("p (k r) -> p k r", r=32)
        parT = rowsT[:, 256:288].rearrange("p (m r) -> p m r", r=8)
        stT = rowsT[:, 288:416].rearrange("p (m r) -> p m r", r=32)

        s_c = sem("s_c")
        s_zero = sem("s_zero")
        s_x = sem("s_x")
        s_con = sem("s_con")
        s_par = sem("s_par")
        s_bm = sem("s_bm")
        s_wg = sem("s_wg")
        s_misc = sem("s_misc")
        landed = [sem(f"landed{i}") for i in range(SLOTS)]
        s_silu = sem("s_silu")
        s_sq = sem("s_sq")
        s_xn = sem("s_xn")
        s_setupT = sem("s_setupT")
        s_rowsT = sem("s_rowsT")
        s_uTp = sem("s_uTp")
        s_mod = sem("s_mod")
        s_modrow = sem("s_modrow")
        s_modTp = sem("s_modTp")
        s_modT = sem("s_modT")
        s_uTa = sem("s_uTa")
        s_uTd = sem("s_uTd")
        s_xr = sem("s_xr")
        s_xre = sem("s_xre")
        s_yge = sem("s_yge")
        s_conv = sem("s_conv")
        s_gate = sem("s_gate")
        s_sig = sem("s_sig")
        s_spin = sem("s_spin")
        s_spout = sem("s_spout")
        s_spexp = sem("s_spexp")
        s_spln = sem("s_spln")
        s_tanh = sem("s_tanh")
        s_ix = sem("s_ix")
        s_lru = sem("s_lru")
        s_h = sem("s_h")
        s_hy = sem("s_hy")
        s_tailT = sem("s_tailT")
        s_tail = sem("s_tail")
        s_proj = sem("s_proj")
        s_pe = sem("s_pe")
        s_rot = sem("s_rot")
        s_qkT = sem("s_qkT")
        s_qkTe = sem("s_qkTe")
        s_sc = sem("s_sc")
        s_sm = sem("s_sm")
        s_o = sem("s_o")
        s_kv = sem("s_kv")
        s_st = sem("s_st")
        s_oT = sem("s_oT")
        s_oTe = sem("s_oTe")
        s_oTT = sem("s_oTT")
        s_gg = sem("s_gg")
        s_ob = sem("s_ob")
        s_obT = sem("s_obT")
        s_obTe = sem("s_obTe")
        s_s0 = [sem("s_s0a"), sem("s_s0b")]
        s_vblk = sem("s_vblk")
        s_cross = sem("s_cross")
        s_skv = sem("s_skv")
        s_snew = sem("s_snew")
        s_modst = sem("s_modst")
        s_tab = sem("s_tab")
        s_out = sem("s_out")
        s_msq = sem("s_msq")
        s_x1 = sem("s_x1")
        s_xsq = sem("s_xsq")
        s_u2 = sem("s_u2")
        s_u2T = sem("s_u2T")
        s_u2Te = sem("s_u2Te")
        s_rtr = sem("s_rtr")
        s_lg = sem("s_lg")
        s_gexp = sem("s_gexp")
        s_gin = sem("s_gin")
        s_gates = sem("s_gates")
        s_h1 = sem("s_h1")
        s_h1e = sem("s_h1e")
        s_h2 = sem("s_h2")
        s_hTp = sem("s_hTp")
        s_hTe = sem("s_hTe")
        s_dn = sem("s_dn")
        s_y = sem("s_y")
        s_fsq = sem("s_fsq")
        s_g2 = sem("s_g2")
        s_fin = sem("s_fin")
        s_store = sem("s_store")
        s_ssto = sem("s_ssto")
        s_yout = sem("s_yout")
        s_tl = sem("s_tl")
        s_xrms = sem("s_xrms")
        s_root = sem("s_root")
        s_var = sem("s_var")
        s_dev = sem("s_dev")
        s_msum = sem("s_msum")
        s_mrms = sem("s_mrms")
        s_x1rms = sem("s_x1rms")
        s_frms = sem("s_frms")
        s_vec = sem("s_vec")
        s_act = sem("s_act")
        s_pool = sem("s_pool")

        used = {}
        for p in weight_pieces():
            kind, a, b = p
            if kind == "mod":
                used[p] = (s_mod, KT * a + b + 1)
            elif kind == "in":
                used[p] = (s_xr, MT * (a + 1)) if a < 2 else (s_proj, 4 * (TILES - 1) + a - 1)
            elif kind == "out":
                used[p] = (s_out, TILES)
            elif kind in ("wg", "wu"):
                used[p] = (s_h1, TILES * (a + 1))
            else:
                used[p] = (s_dn, TILES * (a + 1))

        def weights(eng, piece):
            eng.wait_ge(landed[slot[piece]], 16 * nth[piece])
            return ring[:, slot[piece], :]

        def spread(eng, parts, done):
            for name, k in parts:
                eng.dma_start(tab[name + "p"], mod_rows_dram[0:1, k * D:(k + 1) * D]
                              .to_broadcast([P, D])).then_inc(done, 16)
                for b in range(DB):
                    eng.dma_start(tab[name + "s"][b * DT:(b + 1) * DT, :],
                                  mod_rows_dram[1 + b:2 + b, k * D:(k + 1) * D]
                                  .to_broadcast([DT, D])).then_inc(done, 16)

        block = ctx.enter_context(nc.Block())

        @block.sync
        def _(sp):
            for p in weight_pieces():
                kind, a, b = p
                if before[p] is not None:
                    sp.wait_ge(*used[before[p]])
                dst = ring[:, slot[p], :]
                if kind == "mod":
                    src = w_mod[0, b * P:(b + 1) * P, a * 2048:(a + 1) * 2048]
                elif kind in ("in", "out"):
                    w = w_in if kind == "in" else w_out
                    src = w[0, b * 4 * P:(b + 1) * 4 * P, a * 512:(a + 1) * 512].rearrange(
                        "(k p) n -> p k n", p=P)
                    dst = dst.rearrange("p (k n) -> p k n", n=512)
                elif kind == "wd":
                    src = w_exp_down[0, a].rearrange("(k p) n -> p k n", p=P)
                    dst = dst.rearrange("p (k n) -> p k n", n=D)
                else:
                    w = w_exp_gate if kind == "wg" else w_exp_up
                    src = w[0, a].rearrange("(k p) n -> p k n", p=P)
                    dst = dst.rearrange("p (k n) -> p k n", n=FE)
                sp.dma_start(dst, src).then_inc(landed[slot[p]], 16)

        @block.gpsimd
        def _(pool):
            pool.memset(hy[0:32, 0:2, :], 0.0).then_inc(s_zero, 1)
            pool.memset(ss[:], 1.0).then_inc(s_zero, 1)
            pool.memset(eps[:, 0:1], NORM_EPS).then_inc(s_zero, 1)
            pool.memset(eps[:, 1:2], GN_EPS).then_inc(s_zero, 1)
            for i in range(2):
                pool.memset(xr[i][:, 0:3], 0.0).then_inc(s_zero, 1)
            pool.wait_ge(s_zero, 6)
            pool.memset(nm[0:64, 0, :], 1.0).then_inc(s_zero, 1)
            pool.wait_ge(s_zero, 7)
            pool.memset(nm[64:128, 1, :], 1.0).then_inc(s_zero, 1)

            pool.wait_ge(s_zero, 1)
            pool.dma_start(crow[0:1, :], c_prompt).then_inc(s_c, 16)
            pool.dma_start(crow[1:1 + DB, :], c_sample).then_inc(s_c, 16)
            for r in range(CONVW):
                pool.dma_start(par[r:r + 1, :], conv_w[0, r:r + 1, :]).then_inc(s_par, 16)
            pool.dma_start(par[4:5, :], conv_b).then_inc(s_par, 16)
            pool.dma_start(par[5:6, :], b_rgate.rearrange("a n k -> a (n k)")).then_inc(s_par, 16)
            pool.dma_start(par[6:7, :], b_igate.rearrange("a n k -> a (n k)")).then_inc(s_par, 16)
            pool.dma_start(par[7:8, :], lru_lambda).then_inc(s_par, 16)
            pool.dma_start(srow[0:24, :], state_conv.rearrange("a b w c -> (a b w) c"))\
                .then_inc(s_par, 16)
            pool.dma_start(srow[24:32, :], state_lru[0]).then_inc(s_par, 16)
            for j in range(4):
                pool.dma_start(bm[32 * j:32 * j + 32, :, :],
                               b_mod.rearrange("a (g j n) -> a g j n", g=NMOD, j=4)[:, :, j, :]
                               .to_broadcast([32, NMOD, 512])).then_inc(s_bm, 16)
            for gq, j0, w in ((0, 2, norm_pre_mix), (1, 0, norm_post_mix), (2, 0, norm_pre_ffn),
                              (2, 2, norm_post_ffn)):
                for j in range(2):
                    q0 = 32 * (j0 + j)
                    pool.dma_start(nm[q0:q0 + 32, gq, :], w[0:1, j * 512:(j + 1) * 512]
                                   .to_broadcast([32, 512])).then_inc(s_bm, 16)
            for gi, w in enumerate((w_rgate, w_igate)):
                wv = w[0].rearrange("(m a) j k -> a j m k", a=2)
                for a in range(2):
                    pool.dma_start(wgate[64 * a:64 * a + 64, gi, :, :], wv[a]).then_inc(s_wg, 16)
            pool.dma_start(gnw[:], ret_gn_w.to_broadcast([P, DL])).then_inc(s_misc, 16)
            pool.dma_start(wrt[:, :, 0:NG], w_router_group[0].rearrange("(k p) n -> p k n", p=P))\
                .then_inc(s_misc, 16)
            pool.dma_start(wrt[:, :, NG:], w_router_expert[0].rearrange("(k p) n -> p k n", p=P))\
                .then_inc(s_misc, 16)
            pool.dma_start(brt[:, 0:NG], b_router_group.to_broadcast([P, NG])).then_inc(s_misc, 16)
            pool.dma_start(brt[:, NG:], b_router_expert.to_broadcast([P, NE])).then_inc(s_misc, 16)

            for gq in (1, 2):
                pool.wait_ge(s_modrow, gq + 1)
                for j in range(4):
                    c0 = gq * 2048 + j * 512
                    pool.dma_start(mod_rows_dram[:, c0:c0 + 512], bm[32 * j:32 * j + 1 + DB, gq, :])\
                        .then_inc(s_modst, 16)
            pool.wait_ge(s_modst, 16 * 8)
            pool.wait_ge(s_hy, MT)
            spread(pool, (("g1", 2), ("s2", 3), ("a2", 4)), s_tab)

            pool.wait_ge(s_tail, 1)
            tl = tailrow
            pool.dma_start(conv_prompt.rearrange("a b w c -> (a b w) c"), tl[0:3, :])\
                .then_inc(s_store, 16)
            pool.dma_start(conv_sample.rearrange("a b w c -> (a b w) c"), tl[3:27, :])\
                .then_inc(s_store, 16)
            pool.dma_start(lru_prompt[0], tl[27:28, :]).then_inc(s_store, 16)
            pool.dma_start(lru_sample[0], tl[28:36, :]).then_inc(s_store, 16)
            pool.wait_ge(s_st, TILES - 1)
            pool.dma_start(ret_prompt[0, 0].rearrange("h k e -> k h e"),
                           S.rearrange("p (h e) -> p h e", e=DK)).then_inc(s_store, 16)
            for h in range(NH):
                if h == 0:
                    pool.wait_ge(s_rot, 2 * TILES)
                    pool.wait_ge(s_st, TILES - 1)
                if h >= 2:
                    pool.wait_ge(s_ssto, 16 * (h - 1))
                pool.dma_start(s0[h % 2], state_ret[0, :, h].rearrange("b k e -> k b e"))\
                    .then_inc(s_s0[h % 2], 16)
                pool.wait_ge(s_pe, 4 * TILES)
                if h == 0:
                    pool.wait_ge(s_kv, TILES - 1)
                if h > 0:
                    pool.wait_ge(s_skv, 2 * h)
                pool.tensor_tensor(
                    out=vblk[0:NS], in0=vv[0][0:NS, None, h * DK:(h + 1) * DK].to_broadcast([NS, DB, DK]),
                    in1=con[0:NS, C_BM:C_BM + DB].unsqueeze(2).to_broadcast([NS, DB, DK]),
                    op=ALU.mult).then_inc(s_vblk, 1)
                if h >= 1:
                    pool.wait_ge(s_snew, 2 * h)
                    pool.dma_start(ret_sample[0, :, h - 1].rearrange("b k e -> k b e"),
                                   s0[(h - 1) % 2]).then_inc(s_ssto, 16)
            pool.wait_ge(s_snew, 2 * NH)
            pool.dma_start(ret_sample[0, :, NH - 1].rearrange("b k e -> k b e"),
                           s0[(NH - 1) % 2]).then_inc(s_ssto, 16)
            pool.wait_ge(s_u2, TILES)
            spread(pool, (("g2", 5),), s_g2)
            pool.wait_ge(s_store, 16 * 5)
            pool.wait_ge(s_ssto, 16 * NH)


        @block.tensor
        def _(pe):
            def mm(out, lhsT, rhs, first, last):
                return nc.tensor.matmul(out, lhsT, rhs, start=first, stop=last)

            def turn(out, src):
                return nc.tensor.transpose(out, src, ident[0:src.shape[0], 0:src.shape[0]])

            pe.wait_ge(s_con, 16)
            pe.wait_ge(s_silu, 1)
            pe.wait_ge(s_par, 16 * 10)
            for k in range(KT):
                turn(bank[0][:, 32 * k:32 * k + 32], crow[:, k * P:(k + 1) * P])
            for m in range(MT):
                turn(bank[0][:, 256 + 8 * m:264 + 8 * m], par[:, m * P:(m + 1) * P])
            for m in range(MT):
                last = turn(bank[0][:, 288 + 32 * m:320 + 32 * m], srow[:, m * P:(m + 1) * P])
            last.then_inc(s_setupT, 1)

            def turn_x(k, b):
                for t in range(TILES - 1):
                    last = turn(bank[b][:, t * P:(t + 1) * P], xn[:, t, k * P:(k + 1) * P])
                last.then_inc(s_uTp, 1)

            pe.wait_ge(s_xn, TILES)
            for k in range(7):
                turn_x(k, k + 1)

            def mod_step(gq, k, b):
                w = weights(pe, ("mod", gq, k))
                for j in range(4):
                    last = mm(bank[b][32 * j:32 * j + 32, :], cT[:, k, :],
                              w[:, j * 512:(j + 1) * 512], k == 0, k == KT - 1)
                last.then_inc(s_mod, 1)

            pe.wait_ge(s_rowsT, 1)
            for k in range(KT):
                mod_step(0, k, 0)
            pe.wait_ge(s_modrow, 1)
            for q in range(4):
                last = turn(bank[0][:, q * P:(q + 1) * P], bm[:, 0, q * P:(q + 1) * P])
            last.then_inc(s_modTp, 1)
            pe.wait_ge(s_uTa, 1)
            turn_x(7, 1)
            pe.wait_ge(s_uTd, 1)
            for k in range(KT):
                last = nc.tensor.transpose(bank[2][:, k * NS:(k + 1) * NS],
                                           xn[0:NS, TILES - 1, k * P:(k + 1) * P], ident[0:NS, 0:NS])
            last.then_inc(s_uTp, 1)

            half = NTOK // 2

            def by_channel(c, m):
                i = MT * c + m
                w = [weights(pe, ("in", c, h)).rearrange("p (k n) -> p k n", n=512) for h in range(2)]
                if i == 0:
                    pe.wait_ge(s_uTa, 4)
                    pe.wait_ge(s_uTd, 5)
                if i >= 2:
                    if i - 2 < MT:
                        pe.wait_ge(s_xre, i - 1)
                    else:
                        pe.wait_ge(s_yge, i - 1 - MT)
                for n in range(2):
                    for k in range(KT):
                        last = mm(bank[2 * (i % 2) + n][:, 0:half],
                                  w[k // 4][:, k % 4, m * P:(m + 1) * P],
                                  uT[:, k, n * half:(n + 1) * half], k == 0, k == KT - 1)
                last.then_inc(s_xr, 1)

            def gate_products(m):
                pe.wait_ge(s_conv, m + 1)
                pe.wait_ge(s_wg, 16 * 4)
                if m >= 1:
                    pe.wait_ge(s_sig, 2 * m)
                for gi in range(2):
                    for a in range(2):
                        q = slice(64 * a, 64 * a + 64)
                        mm(bank[5 + gi][q, :], wgate[q, gi, m, :], xc[m % 2][q, 0:SEQ], True, True)
                    for a in range(2):
                        q = slice(64 * a, 64 * a + 64)
                        last = mm(bank[7][q, gi * NS:(gi + 1) * NS], wgate[q, gi, m, :],
                                  xc[m % 2][q, SEQ:NTOK], True, True)
                last.then_inc(s_gate, 1)

            by_channel(0, 0)
            mod_step(1, 0, 4)
            mod_step(1, 1, 4)
            by_channel(0, 1)
            mod_step(1, 2, 4)
            mod_step(1, 3, 4)
            gate_products(0)
            by_channel(0, 2)
            mod_step(1, 4, 4)
            mod_step(1, 5, 4)
            gate_products(1)
            by_channel(0, 3)
            mod_step(1, 6, 4)
            mod_step(1, 7, 4)
            gate_products(2)
            by_channel(1, 0)
            pe.wait_ge(s_modrow, 2)
            mod_step(2, 0, 4)
            mod_step(2, 1, 4)
            gate_products(3)
            for m in range(1, MT):
                by_channel(1, m)
                mod_step(2, 2 * m, 4)
                mod_step(2, 2 * m + 1, 4)
            pe.wait_ge(s_h, MT)
            pe.wait_ge(s_sig, 2 * MT)
            for m in range(MT):
                last = turn(bank[7][0:36, m * P:(m + 1) * P], tails[:, m, :])
            last.then_inc(s_tailT, 1)

            def project(t, c):
                w = [weights(pe, ("in", 2 + c, h)).rearrange("p (k n) -> p k n", n=512)
                     for h in range(2)]
                n = rows(t)
                if t == 0:
                    pe.wait_ge(s_yge, 3 + (c >= 2))
                else:
                    pe.wait_ge(s_pe, 4 * (t - 1) + c + 1)
                for k in range(KT):
                    last = mm(bank[c][0:n, :], uT[:, k, t * P:t * P + n], w[k // 4][:, k % 4, :],
                              k == 0, k == KT - 1)
                last.then_inc(s_proj, 1)

            def turn_qk(t):
                n = rows(t)
                pe.wait_ge(s_rot, 2 * t + 2)
                if t == 0:
                    pe.wait_ge(s_modrow, 3)
                    pe.wait_ge(s_sig, 2 * MT)
                else:
                    pe.wait_ge(s_obTe, t)
                    pe.wait_ge(s_st, t)
                for b, src in ((4, qr), (5, kr[t % 2])):
                    for h in range(NH):
                        last = turn(bank[b][:, h * P:h * P + n], src[0:n, h * P:(h + 1) * P])
                last.then_inc(s_qkT, 1)

            def scores(t):
                n = rows(t)
                pe.wait_ge(s_qkTe, t + 1)
                if t >= 1:
                    pe.wait_ge(s_sm, t)
                for h in range(NH):
                    last = mm(bank[6][0:n, h * n:(h + 1) * n], kT[:, h * P:h * P + n],
                              qT[:, h * P:h * P + n], True, True)
                last.then_inc(s_sc, 1)

            def outputs(t):
                pe.wait_ge(s_sm, t + 1)
                pe.wait_ge(s_pe, 4 * t + 3)
                if t == 0:
                    pe.wait_ge(s_tail, 1)
                else:
                    pe.wait_ge(s_ob, t)
                    pe.wait_ge(s_st, t)
                for h in range(NH):
                    c = slice(h * P, (h + 1) * P)
                    last = mm(bank[7][:, c], sm[:, c], vv[t % 2][:, c], True, t == 0)
                    if t:
                        last = mm(bank[7][:, c], qT[:, c], S[:, c], False, True)
                last.then_inc(s_o, 1)
                for h in range(NH):
                    c = slice(h * P, (h + 1) * P)
                    last = mm(bank[5][:, c], kr[t % 2][:, c], vv[t % 2][:, c], True, True)
                last.then_inc(s_kv, 1)

            def turn_out(t):
                n = rows(t)
                pe.wait_ge(s_ob, t + 1)
                for h in range(NH):
                    last = turn(bank[4][:, h * P:h * P + n], ob[0:n, h * P:(h + 1) * P])
                last.then_inc(s_obT, 1)

            def sample_outputs():
                t = TILES - 1
                pe.wait_ge(s_sm, t + 1)
                pe.wait_ge(s_pe, 4 * t + 3)
                pe.wait_ge(s_ob, t)
                for h in range(NH):
                    c = slice(h * DK, (h + 1) * DK)
                    o = bank[7][:, h * NS:(h + 1) * NS]
                    pe.wait_ge(s_s0[h % 2], 16 * (h // 2 + 1))
                    mm(o, vv[0][0:NS, c], sm[0:NS, h * NS:(h + 1) * NS], True, False)
                    for b in range(DB):
                        q0 = h * P + b * DT
                        last = mm(o[:, b * DT:(b + 1) * DT], s0[h % 2][:, b, :], qT[:, q0:q0 + DT],
                                  False, b == DB - 1)
                    last.then_inc(s_cross, 1)
                    pe.wait_ge(s_vblk, h + 1)
                    for n in range(2):
                        i = 2 * h + n
                        if i >= 2:
                            pe.wait_ge(s_snew, i - 1)
                        elif i == 0:
                            pe.wait_ge(s_obTe, t)
                        mm(bank[4 + n][:], kr[0][0:NS, c],
                           vblk[0:NS, 4 * n:4 * n + 4, :].rearrange("p b e -> p (b e)"),
                           True, True).then_inc(s_skv, 1)
                pe.wait_ge(s_oTe, 1)
                for h in range(NH):
                    last = turn(bank[6][0:NS, h * P:(h + 1) * P], sm[:, h * NS:(h + 1) * NS])
                last.then_inc(s_o, 1)

            for t in range(TILES + 1):
                steps = [lambda: turn_qk(t - 1), lambda: scores(t - 1), lambda: outputs(t - 1),
                         lambda: turn_out(t - 1)]
                if t == TILES:
                    steps[2] = sample_outputs
                for c in range(4):
                    if t < TILES:
                        project(t, c)
                    if t == TILES and c == 3:
                        pe.wait_ge(s_snew, 2 * NH)
                    if t:
                        steps[c]()

            def out_proj(t):
                n = rows(t)
                if t == 0:
                    pe.wait_ge(s_pe, 4 * TILES)
                    pe.wait_ge(s_obTe, TILES)
                if t >= 2:
                    pe.wait_ge(s_x1, t - 1)
                for c in range(2):
                    for k in range(KT):
                        w = weights(pe, ("out", c, k // 4)).rearrange("p (k n) -> p k n", n=512)
                        src = hy[:, k] if k < MT else outbT[:, k - MT]
                        last = mm(bank[2 * (t % 2) + c][0:n, :], src[:, t * P:t * P + n],
                                  w[:, k % 4, :], k == 0, k == KT - 1)
                last.then_inc(s_out, 1)

            def turn_u2(t):
                n = rows(t)
                pe.wait_ge(s_u2, t + 1)
                if t == 0:
                    pe.wait_ge(s_snew, 2 * NH)
                else:
                    pe.wait_ge(s_u2Te, 2 * t)
                for hf in range(2):
                    for k in range(4):
                        last = turn(bank[4 + hf][:, k * P:k * P + n],
                                    u2[t % 2][0:n, (4 * hf + k) * P:(4 * hf + k + 1) * P])
                    last.then_inc(s_u2T, 1)
                pe.wait_ge(s_u2Te, 2 * t + 2)
                pe.wait_ge(s_misc, 16 * 5)
                if t == 0:
                    pe.wait_ge(s_ob, TILES)
                else:
                    pe.wait_ge(s_lg, t)
                for k in range(KT):
                    last = mm(bank[6][0:n, 0:NG + NE], uT[:, k, t * P:t * P + n], wrt[:, k, :],
                              k == 0, k == KT - 1)
                last.then_inc(s_rtr, 1)

            for t in range(TILES + 1):
                if t < TILES:
                    out_proj(t)
                if t:
                    turn_u2(t - 1)

            def expert_in(i):
                e, t = divmod(i, TILES)
                n = rows(t)
                wg = weights(pe, ("wg", e, 0)).rearrange("p (k n) -> p k n", n=FE)
                wu = weights(pe, ("wu", e, 0)).rearrange("p (k n) -> p k n", n=FE)
                if i < 2:
                    pe.wait_ge(s_x1, TILES)
                else:
                    pe.wait_ge(s_h2, i - 1)
                for j, w in enumerate((wg, wu)):
                    for k in range(KT):
                        last = mm(bank[i % 2][0:n, j * FE:(j + 1) * FE], uT[:, k, t * P:t * P + n],
                                  w[:, k, :], k == 0, k == KT - 1)
                last.then_inc(s_h1, 1)

            def expert_out(i):
                e, t = divmod(i, TILES)
                n = rows(t)
                wd = weights(pe, ("wd", e, 0)).rearrange("p (k n) -> p k n", n=D)
                pe.wait_ge(s_h2, i + 1)
                if i >= 1:
                    pe.wait_ge(s_hTe, i)
                else:
                    pe.wait_ge(s_x1, TILES)
                for k in range(FT):
                    last = turn(bank[2][:, k * P:k * P + n], hg[i % 2][0:n, k * P:(k + 1) * P])
                last.then_inc(s_hTp, 1)
                pe.wait_ge(s_hTe, i + 1)
                if i >= 2:
                    pe.wait_ge(s_y, i - 1)
                elif i == 0:
                    pe.wait_ge(s_lg, TILES)
                    pe.wait_ge(s_u2Te, 2 * TILES)
                for c in range(2):
                    for k in range(FT):
                        last = mm(bank[4 + 2 * (i % 2) + c][0:n, :], hT[i % 2][:, k * P:k * P + n],
                                  wd[:, k, c * 512:(c + 1) * 512], k == 0, k == FT - 1)
                last.then_inc(s_dn, 1)

            for i in range(NE * TILES + 1):
                if i < NE * TILES:
                    expert_in(i)
                if i:
                    expert_out(i - 1)

        @block.scalar
        def _(act):
            def f(out, src, func, done, **kw):
                return nc.scalar.activation(out, src, func, **kw).then_inc(done, 1)

            act.dma_start(x[:, 0:TILES - 1, :], x_prompt[0].rearrange("(t p) d -> p t d", p=P))\
                .then_inc(s_x, 16)
            act.dma_start(x[0:NS, TILES - 1, :], x_sample.rearrange("b t d -> (b t) d"))\
                .then_inc(s_x, 16)
            act.dma_start(con[:], consts).then_inc(s_con, 16)

            act.wait_ge(s_c, 32)
            f(crow, crow, ACT.Silu, s_silu)
            act.wait_ge(s_zero, 4)
            act.wait_ge(s_x, 32)
            for t in range(TILES):
                n = rows(t)
                f(xn[0:n, t], x[0:n, t], ACT.Square, s_sq, accum_out=ss[0:n, 0, t, 0:1])
            act.wait_ge(s_sq, TILES)
            f(ss[:, 0, :, 0], ss[:, 0, :, 0], ACT.Sqrt, s_xrms, scale=1.0 / D, bias=eps[:, 0:1])
            act.wait_ge(s_spin, 1)
            f(softp[:, 1], softp[:, 0], ACT.Exp, s_spexp, scale=-1.0)
            act.wait_ge(s_spin, 2)
            f(softp[:, 3], softp[:, 2], ACT.Ln, s_spln)

            act.wait_ge(s_modT, 1)
            act.wait_ge(s_uTp, 7)
            for k in range(0, KT, 2):
                f(uT[:, k, 0:SEQ], bank[k % 7 + 1][:], ACT.Identity, s_uTa,
                  scale=modT[:, k % 4, 2 + k // 4, 0:1], bias=modT[:, k % 4, k // 4, 0:1])

            half = NTOK // 2

            def take_xr(m):
                b = xr[m % 2]
                smp = b[:, 3 + SEQ:].rearrange("p (b t) -> p b t", t=3 + DT)
                act.wait_ge(s_xr, m + 1)
                if m >= 2:
                    act.wait_ge(s_conv, m - 1)
                b0, b1 = bank[2 * (m % 2)], bank[2 * (m % 2) + 1]
                f(b[:, 3:3 + half], b0[:, 0:half], ACT.Copy, s_act)
                f(b[:, 3 + half:3 + SEQ], b1[:, 0:SEQ - half], ACT.Copy, s_act)
                f(smp[:, :, 3:], b1[:, SEQ - half:half].rearrange("p (b t) -> p b t", t=DT),
                  ACT.Copy, s_act)
                f(smp[:, :, 0:3], stT[:, m, 0:24].rearrange("p (b t) -> p b t", t=3),
                  ACT.Copy, s_xre)

            def sigmoids(m):
                act.wait_ge(s_gate, m + 1)
                if m >= 1:
                    act.wait_ge(s_lru, m)
                for gi, buf in ((0, R), (1, I)):
                    f(buf[:, 0:SEQ], bank[5 + gi][:], ACT.Sigmoid, s_act,
                      bias=parT[:, m, 5 + gi:6 + gi])
                    f(buf[:, SEQ:], bank[7][:, gi * NS:(gi + 1) * NS], ACT.Sigmoid, s_sig,
                      bias=parT[:, m, 5 + gi:6 + gi])
                act.wait_ge(s_sig, 2 * m + 2)
                if m == 0:
                    act.wait_ge(s_spout, 1)
                f(R, R, ACT.Tanh, s_tanh, scale=softp[:, 7, m:m + 1])
                act.wait_ge(s_tanh, m + 1)
                f(Z, R, ACT.Sqrt, s_root, scale=-1.0)

            def gelus(m):
                i = MT + m
                act.wait_ge(s_xr, i + 1)
                if m >= 1:
                    act.wait_ge(s_lru, MT)
                if m >= 2:
                    act.wait_ge(s_hy, m - 1)
                for n in range(2):
                    f(ge[m % 2][:, n * half:(n + 1) * half], bank[2 * (i % 2) + n][:, 0:half],
                      ACT.Gelu_apprx_tanh, s_act if n == 0 else s_yge)

            take_xr(0)
            take_xr(1)
            sigmoids(0)
            take_xr(2)
            sigmoids(1)
            take_xr(3)
            sigmoids(2)
            gelus(0)
            sigmoids(3)
            for m in range(1, MT):
                gelus(m)
            act.wait_ge(s_tailT, 1)
            f(tailrow[:], bank[7][0:36, :], ACT.Copy, s_tail)

            def take(t, c):
                n = rows(t)
                kind = NH * (t == TILES - 1)
                act.wait_ge(s_proj, 4 * t + c + 1)
                if c < 2:
                    dst, col = ((qs, C_DQ), (ks, C_DK))[c]
                    act.wait_ge(s_rot, 2 * t - 1 + c) if t else None
                    for h in range(NH):
                        f(dst[0:n, h * P:(h + 1) * P], bank[c][0:n, h * P:(h + 1) * P], ACT.Copy,
                          s_act if h < NH - 1 else s_pe,
                          scale=con[0:n, col + kind + h:col + kind + h + 1])
                elif c == 2:
                    if t >= 2:
                        act.wait_ge(s_kv, t - 1)
                    f(vv[t % 2][0:n], bank[c][0:n], ACT.Copy, s_pe)
                else:
                    if t >= 2:
                        act.wait_ge(s_ob, t - 1)
                    f(gg[t % 2][0:n], bank[c][0:n], ACT.Silu, s_pe)

            def take_qkT(t):
                n = rows(t)
                act.wait_ge(s_qkT, t + 1)
                if t:
                    act.wait_ge(s_o, t)
                for dst, b in ((qT, 4), (kT, 5)):
                    f(dst.rearrange("p (h i) -> p h i", i=P)[:, :, 0:n],
                      bank[b][:].rearrange("p (h i) -> p h i", i=P)[:, :, 0:n], ACT.Copy,
                      s_act if b == 4 else s_qkTe)

            def take_obT(t):
                n = rows(t)
                act.wait_ge(s_obT, t + 1)
                f(outbT[:, :, t * P:t * P + n],
                  bank[4][:].rearrange("p (h i) -> p h i", i=P)[:, :, 0:n], ACT.Copy, s_obTe)

            def deviation(t):
                n = rows(t)
                act.wait_ge(s_var, t + 1)
                f(grs[0:n], gmv[0:n, :, 1], ACT.Sqrt, s_dev, bias=eps[0:n, 1:2])

            act.wait_ge(s_modst, 16 * 8)
            for t in range(TILES + 1):
                for c in range(4):
                    if t < TILES:
                        take(t, c)
                    if t and c == 0:
                        take_qkT(t - 1)
                    if t == TILES and c == 2:
                        act.wait_ge(s_cross, NH)
                        f(sm[:, 0:NH * NS], bank[7][:, 0:NH * NS], ACT.Copy, s_oTe)
                    if t and c == 3:
                        deviation(t - 1)
                        take_obT(t - 1)

            def square_m(t):
                n = rows(t)
                act.wait_ge(s_out, t + 1)
                for c in range(2):
                    f(junk[0:n, c * 512:(c + 1) * 512], bank[2 * (t % 2) + c][0:n], ACT.Square,
                      s_msq, accum_out=ss[0:n, 1, t, c:c + 1])
                act.wait_ge(s_msq, 2 * t + 2)
                f(ss[0:n, 1, t, 1:2], ss[0:n, 1, t, 1:2], ACT.Identity, s_msum, scale=1.0 / D,
                  bias=eps[0:n, 0:1])
                act.wait_ge(s_msum, t + 1)
                f(ss[0:n, 1, t, 0:1], ss[0:n, 1, t, 0:1], ACT.Sqrt, s_mrms, scale=1.0 / D,
                  bias=ss[0:n, 1, t, 1:2])

            def square_x(t):
                n = rows(t)
                act.wait_ge(s_x1, t + 1)
                f(junk[0:n], x[0:n, t], ACT.Square, s_xsq, accum_out=ss[0:n, 2, t, 0:1])
                act.wait_ge(s_xsq, t + 1)
                f(ss[0:n, 2, t, 0:1], ss[0:n, 2, t, 0:1], ACT.Sqrt, s_x1rms, scale=1.0 / D,
                  bias=eps[0:n, 0:1])

            def take_u2T(t):
                n = rows(t)
                for hf in range(2):
                    act.wait_ge(s_u2T, 2 * t + hf + 1)
                    f(uT[:, 4 * hf:4 * hf + 4, t * P:t * P + n],
                      bank[4 + hf][:].rearrange("p (k i) -> p k i", i=P)[:, :, 0:n], ACT.Copy,
                      s_u2Te)

            for t in range(TILES + 1):
                if t < TILES:
                    square_m(t)
                    square_x(t)
                if t:
                    take_u2T(t - 1)

            act.wait_ge(s_gin, 1)
            f(gx[:, :, 0:NG], gx[:, :, 0:NG], ACT.Exp, s_gexp)
            act.wait_ge(s_gin, 2)
            f(gx[:, :, 4:5], gx[:, :, 4:5], ACT.Exp, s_gexp)

            for i in range(NE * TILES + 1):
                if i < NE * TILES:
                    n = rows(i % TILES)
                    act.wait_ge(s_h1, i + 1)
                    if i >= 2:
                        act.wait_ge(s_h2, i - 1)
                    f(hb[i % 2][0:n], bank[i % 2][0:n, 0:FE], ACT.Silu, s_h1e)
                if i:
                    n = rows((i - 1) % TILES)
                    act.wait_ge(s_hTp, i)
                    if i >= 3:
                        act.wait_ge(s_dn, i - 2)
                    f(hT[(i - 1) % 2].rearrange("p (k i) -> p k i", i=P)[:, :, 0:n],
                      bank[2][:, 0:FE].rearrange("p (k i) -> p k i", i=P)[:, :, 0:n], ACT.Copy,
                      s_hTe)
            act.wait_ge(s_y, NE * TILES)
            for t in range(TILES):
                n = rows(t)
                f(yj[0:n], Y[0:n, t], ACT.Square, s_fsq, accum_out=ss[0:n, 3, t, 0:1])
                act.wait_ge(s_fsq, t + 1)
                f(ss[0:n, 3, t, 0:1], ss[0:n, 3, t, 0:1], ACT.Sqrt, s_frms, scale=1.0 / D,
                  bias=eps[0:n, 0:1])
            for t in range(TILES):
                act.wait_ge(s_fin, t + 1)
                dst = (y_prompt[0, t * P:(t + 1) * P, :] if t < TILES - 1
                       else y_sample.rearrange("b t d -> (b t) d"))
                act.dma_start(dst, x[0:rows(t), t, :]).then_inc(s_yout, 16)
            act.wait_ge(s_yout, 16 * TILES)

        @block.vector
        def _(dve):
            v = nc.vector
            count = [0]

            def link(ins):
                count[0] += 1
                ins.then_inc(s_vec, 1)
                dve.wait_ge(s_vec, count[0])

            dve.wait_ge(s_setupT, 1)
            v.tensor_copy(rowsT[:], bank[0][:, 0:416]).then_inc(s_rowsT, 1)
            dve.wait_ge(s_rowsT, 1)
            lam = parT[:, :, 7]
            v.scalar_tensor_tensor(out=softp[:, 0], in0=lam, scalar=-1.0, in1=lam, op0=ALU.mult,
                                   op1=ALU.max).then_inc(s_spin, 1)

            dve.wait_ge(s_xrms, 1)
            link(v.reciprocal(ss[:, 0, :, 0], ss[:, 0, :, 0]))
            for t in range(TILES):
                n = rows(t)
                v.tensor_scalar(xn[0:n, t], x[0:n, t], ss[0:n, 0, t, 0:1], None, ALU.mult)\
                    .then_inc(s_xn, 1)

            dve.wait_ge(s_spexp, 1)
            v.tensor_scalar(softp[:, 2], softp[:, 1], 1.0, None, ALU.add).then_inc(s_spin, 1)
            dve.wait_ge(s_spin, 2)
            link(v.tensor_scalar(softp[:, 4], softp[:, 2], -1.0, None, ALU.add))
            link(v.tensor_scalar(softp[:, 5], softp[:, 4], 0.0, None, ALU.is_equal))
            link(v.tensor_tensor(out=softp[:, 4], in0=softp[:, 4], in1=softp[:, 5], op=ALU.add))
            link(v.reciprocal(softp[:, 4], softp[:, 4]))
            dve.wait_ge(s_spln, 1)
            link(v.tensor_tensor(out=softp[:, 3], in0=softp[:, 3], in1=softp[:, 5], op=ALU.add))
            link(v.tensor_tensor(out=softp[:, 3], in0=softp[:, 3], in1=softp[:, 4], op=ALU.mult))
            link(v.tensor_tensor(out=softp[:, 3], in0=softp[:, 3], in1=softp[:, 1], op=ALU.mult))
            link(v.tensor_scalar(softp[:, 6], lam, -1.0, 0.0, ALU.mult, ALU.max))
            link(v.tensor_tensor(out=softp[:, 6], in0=softp[:, 6], in1=softp[:, 3], op=ALU.add))
            v.tensor_scalar(softp[:, 7], softp[:, 6], -4.0, None, ALU.mult).then_inc(s_spout, 1)

            def mod_rows(gq, b):
                if gq == 0:
                    dve.wait_ge(s_bm, 16 * 12)
                    dve.wait_ge(s_zero, 8)
                    link(v.tensor_scalar(bm[64:128, 0, :], bm[64:128, 0, :], 1.0, None, ALU.add))
                    link(v.tensor_scalar(bm[0:64, 2, :], bm[0:64, 2, :], 1.0, None, ALU.add))
                dve.wait_ge(s_mod, KT * (gq + 1))
                link(v.tensor_tensor(out=bm[:, gq], in0=bank[b][:], in1=bm[:, gq], op=ALU.add))
                v.tensor_tensor(out=bm[:, gq], in0=bm[:, gq], in1=nm[:, gq], op=ALU.mult)\
                    .then_inc(s_modrow, 1)

            mod_rows(0, 0)
            dve.wait_ge(s_modTp, 1)
            v.tensor_copy(modT[:].rearrange("p a b c -> p (a b c)"), bank[0][:]).then_inc(s_modT, 1)

            dve.wait_ge(s_modT, 1)
            for k in range(1, KT, 2):
                if k == 7:
                    dve.wait_ge(s_uTp, 8)
                v.tensor_scalar(uT[:, k, 0:SEQ], bank[k % 7 + 1][:],
                                modT[:, k % 4, 2 + k // 4, 0:1], modT[:, k % 4, k // 4, 0:1],
                                ALU.mult, ALU.add).then_inc(s_uTd, 1)
            dve.wait_ge(s_uTp, 9)
            for j in range(2):
                u = uT[:, 4 * j:4 * j + 4, SEQ:NTOK]
                for q in range(4):
                    row = lambda jj: modT[:, q, jj, 1:1 + DB].unsqueeze(2).to_broadcast([P, DB, DT])
                    uq = u[:, q].rearrange("p (b t) -> p b t", t=DT)
                    link(v.tensor_tensor(
                        out=uq, in0=bank[2][:, (4 * j + q) * NS:(4 * j + q + 1) * NS].rearrange(
                            "p (b t) -> p b t", t=DT), in1=row(2 + j), op=ALU.mult))
                    last = v.tensor_tensor(out=uq, in0=uq, in1=row(j), op=ALU.add)
                    link(last) if (j, q) != (1, 3) else last.then_inc(s_uTd, 1)

            def conv(m):
                b, o = xr[m % 2], xc[m % 2]
                smp = b[:, 3 + SEQ:].rearrange("p (b t) -> p b t", t=3 + DT)
                osm = o[:, SEQ:].rearrange("p (b t) -> p b t", t=DT)
                dve.wait_ge(s_xre, m + 1)
                if m >= 2:
                    dve.wait_ge(s_lru, m - 1)
                v.tensor_copy(tails[:, m, 0:3], b[:, SEQ:SEQ + 3]).then_inc(s_tl, 1)
                v.tensor_copy(tails[:, m, 3:27].rearrange("p (b t) -> p b t", t=3), smp[:, :, DT:])\
                    .then_inc(s_tl, 1)
                v.tensor_scalar(o[:, 0:SEQ], b[:, 0:SEQ], parT[:, m, 0:1], parT[:, m, 4:5],
                                ALU.mult, ALU.add)
                link(v.tensor_scalar(osm, smp[:, :, 0:DT], parT[:, m, 0:1], parT[:, m, 4:5],
                                     ALU.mult, ALU.add))
                for j in range(1, CONVW):
                    v.scalar_tensor_tensor(out=o[:, 0:SEQ], in0=b[:, j:j + SEQ],
                                           scalar=parT[:, m, j:j + 1], in1=o[:, 0:SEQ],
                                           op0=ALU.mult, op1=ALU.add)
                    last = v.scalar_tensor_tensor(out=osm, in0=smp[:, :, j:j + DT],
                                                  scalar=parT[:, m, j:j + 1], in1=osm,
                                                  op0=ALU.mult, op1=ALU.add)
                    link(last) if j < CONVW - 1 else last.then_inc(s_conv, 1)

            def rg_lru(m):
                dve.wait_ge(s_sig, 2 * m + 2)
                dve.wait_ge(s_conv, m + 1)
                link(v.tensor_tensor(out=I, in0=I, in1=xc[m % 2], op=ALU.mult))
                dve.wait_ge(s_tanh, m + 1)
                link(v.tensor_scalar(Q, R, -1.0, 1.0, ALU.mult, ALU.add))
                link(v.reciprocal(Q, Q))
                link(v.scalar_tensor_tensor(out=A, in0=R, scalar=1.0, in1=Q, op0=ALU.add,
                                            op1=ALU.mult))
                dve.wait_ge(s_root, m + 1)
                link(v.scalar_tensor_tensor(out=Q, in0=Z, scalar=2.0, in1=Q, op0=ALU.mult,
                                            op1=ALU.mult))
                link(v.tensor_tensor(out=I, in0=I, in1=Q, op=ALU.mult))
                A0 = A[:, SEQ:].rearrange("p (b t) -> p b t", t=DT)[:, :, 0]
                I0 = I[:, SEQ:].rearrange("p (b t) -> p b t", t=DT)[:, :, 0]
                link(v.tensor_tensor(out=Q[:, 0:DB], in0=A0, in1=stT[:, m, 24:32], op=ALU.mult))
                link(v.tensor_tensor(out=I0, in0=I0, in1=Q[:, 0:DB], op=ALU.add))
                link(v.tensor_scalar(A0, A0, 0.0, None, ALU.mult))
                v.tensor_tensor_scan(hy[:, m], A, I, 0.0, ALU.mult, ALU.add).then_inc(s_lru, 1)
                dve.wait_ge(s_lru, m + 1)
                v.tensor_copy(tails[:, m, 27:28], hy[:, m, SEQ - 1:SEQ]).then_inc(s_tl, 1)
                v.tensor_copy(tails[:, m, 28:36],
                              hy[:, m, SEQ:].rearrange("p (b t) -> p b t", t=DT)[:, :, DT - 1])\
                    .then_inc(s_h, 1)

            def gated(m):
                dve.wait_ge(s_yge, m + 1)
                dve.wait_ge(s_h, m + 1)
                v.tensor_tensor(out=hy[:, m], in0=hy[:, m], in1=ge[m % 2], op=ALU.mult)\
                    .then_inc(s_hy, 1)

            conv(0)
            conv(1)
            rg_lru(0)
            conv(2)
            rg_lru(1)
            conv(3)
            mod_rows(1, 4)
            rg_lru(2)
            gated(0)
            rg_lru(3)
            for m in range(1, MT):
                gated(m)
            mod_rows(2, 4)

            def rotate(t, c):
                n = rows(t)
                src, dst = ((qs, qr), (ks, kr[t % 2]))[c]
                halves = lambda r: r[0:n].rearrange("p (h z d) -> p h z d", z=2, d=64)
                cs = cosv[0:n, t][:, None, :].to_broadcast([n, 2 * NH, 64])
                sn = sinv[0:n, t][:, None, :].to_broadcast([n, NH, 64])
                dve.wait_ge(s_pe, 4 * t + c + 1)
                if t or c:
                    dve.wait_ge(s_rot, 2 * t + c)
                if c == 0 and t:
                    dve.wait_ge(s_qkT, t)
                if c == 1 and t >= 2:
                    dve.wait_ge(s_kv, t - 1)
                v.tensor_tensor(out=dst[0:n].rearrange("p (h d) -> p h d", d=64),
                                in0=src[0:n].rearrange("p (h d) -> p h d", d=64), in1=cs,
                                op=ALU.mult)
                v.tensor_tensor(out=halves(tB)[:, :, 0], in0=halves(src)[:, :, 1], in1=sn,
                                op=ALU.mult)
                link(v.tensor_tensor(out=halves(tB)[:, :, 1], in0=halves(src)[:, :, 0], in1=sn,
                                     op=ALU.mult))
                link(v.tensor_tensor(out=halves(dst)[:, :, 0], in0=halves(dst)[:, :, 0],
                                     in1=halves(tB)[:, :, 0], op=ALU.subtract))
                v.tensor_tensor(out=halves(dst)[:, :, 1], in0=halves(dst)[:, :, 1],
                                in1=halves(tB)[:, :, 1], op=ALU.add).then_inc(s_rot, 1)

            def mask(t):
                n = rows(t)
                m0 = C_MP if t < TILES - 1 else C_MS
                dve.wait_ge(s_sc, t + 1)
                if t:
                    dve.wait_ge(s_o, t)
                v.tensor_tensor(out=sm[0:n, 0:NH * n].rearrange("p (h i) -> p h i", i=n),
                                in0=bank[6][0:n, 0:NH * n].rearrange("p (h i) -> p h i", i=n),
                                in1=con[0:n, m0:m0 + n][:, None, :].to_broadcast([n, NH, n]),
                                op=ALU.mult).then_inc(s_sm, 1)

            def advance(t):
                dve.wait_ge(s_kv, t + 1)
                dve.wait_ge(s_o, t + 1)
                if t == 0:
                    src = bank[5]
                else:
                    link(v.tensor_tensor(out=tS, in0=S, in1=bank[5][:], op=ALU.add))
                    src = tS
                for h in range(NH):
                    c = slice(h * P, (h + 1) * P)
                    last = v.tensor_scalar(S[:, c], src[:, c], GAMMA_CHUNK[h], None, ALU.mult)
                last.then_inc(s_st, 1)

            def group_norm(t):
                n = rows(t)
                o = bank[7 if t < TILES - 1 else 6]
                dve.wait_ge(s_o, t + 1)
                if t:
                    dve.wait_ge(s_obT, t)
                for h in range(NH):
                    last = v.bn_stats(gst[0:n, h], o[0:n, h * P:(h + 1) * P])
                link(last)
                for h in range(NH):
                    last = v.bn_aggr(gmv[0:n, h], gst[0:n, h])
                last.then_inc(s_var, 1)
                dve.wait_ge(s_dev, t + 1)
                link(v.reciprocal(grs[0:n], grs[0:n]))
                for h in range(NH):
                    c = slice(h * P, (h + 1) * P)
                    last = v.tensor_scalar(ob[0:n, c], o[0:n, c], gmv[0:n, h, 0:1],
                                           grs[0:n, h:h + 1], ALU.subtract, ALU.mult)
                link(last)
                dve.wait_ge(s_gg, t + 1)
                v.tensor_tensor(out=ob[0:n], in0=ob[0:n], in1=gg[t % 2][0:n], op=ALU.mult)\
                    .then_inc(s_ob, 1)

            def gate_weight(t):
                n = rows(t)
                dve.wait_ge(s_pe, 4 * t + 4)
                dve.wait_ge(s_misc, 16 * 5)
                v.tensor_tensor(out=gg[t % 2][0:n], in0=gg[t % 2][0:n], in1=gnw[0:n], op=ALU.mult)\
                    .then_inc(s_gg, 1)

            def sample_states():
                for h in range(NH):
                    dve.wait_ge(s_cross, h + 1)
                    for n in range(2):
                        part = s0[h % 2][:, 4 * n:4 * n + 4, :].rearrange("p b e -> p (b e)")
                        dve.wait_ge(s_skv, 2 * h + n + 1)
                        link(v.tensor_tensor(out=part, in0=part, in1=bank[4 + n][:], op=ALU.add))
                        v.tensor_scalar(part, part, GAMMA_STEP[h], None, ALU.mult)\
                            .then_inc(s_snew, 1)

            for t in range(TILES + 1):
                if t < TILES:
                    rotate(t, 0)
                if t:
                    mask(t - 1)
                if t < TILES:
                    rotate(t, 1)
                if t == TILES:
                    sample_states()
                elif t:
                    advance(t - 1)
                if t:
                    group_norm(t - 1)
                if t < TILES:
                    gate_weight(t)

            tag = lambda t: "p" if t < TILES - 1 else "s"

            def after_mixer(t):
                n = rows(t)
                dve.wait_ge(s_mrms, t + 1)
                link(v.reciprocal(ss[0:n, 1, t, 0:1], ss[0:n, 1, t, 0:1]))
                if t == 0:
                    dve.wait_ge(s_tab, 16 * 27)
                    dve.wait_ge(s_ssto, 16 * NH)
                for c in range(2):
                    w = slice(c * 512, (c + 1) * 512)
                    last = v.scalar_tensor_tensor(
                        out=t1[0:n, w], in0=bank[2 * (t % 2) + c][0:n],
                        scalar=ss[0:n, 1, t, 0:1], in1=tab["g1" + tag(t)][0:n, w], op0=ALU.mult,
                        op1=ALU.mult)
                link(last)
                v.tensor_tensor(out=x[0:n, t], in0=x[0:n, t], in1=t1[0:n], op=ALU.add)\
                    .then_inc(s_x1, 1)
                dve.wait_ge(s_x1rms, t + 1)
                link(v.reciprocal(ss[0:n, 2, t, 0:1], ss[0:n, 2, t, 0:1]))
                if t >= 2:
                    dve.wait_ge(s_u2T, 2 * (t - 1))
                link(v.scalar_tensor_tensor(
                    out=u2[t % 2][0:n], in0=x[0:n, t], scalar=ss[0:n, 2, t, 0:1],
                    in1=tab["a2" + tag(t)][0:n], op0=ALU.mult, op1=ALU.mult))
                v.tensor_tensor(out=u2[t % 2][0:n], in0=u2[t % 2][0:n],
                                in1=tab["s2" + tag(t)][0:n], op=ALU.add).then_inc(s_u2, 1)

            def take_logits(t):
                n = rows(t)
                dve.wait_ge(s_rtr, t + 1)
                v.tensor_tensor(out=logit[0:n, t], in0=bank[6][0:n, 0:NG + NE], in1=brt[0:n],
                                op=ALU.add).then_inc(s_lg, 1)

            v.memset(logit[:], 0.0).then_inc(s_tl, 1)
            dve.wait_ge(s_tl, 3 * MT + 1)
            for t in range(TILES + 1):
                if t < TILES:
                    after_mixer(t)
                if t:
                    take_logits(t - 1)

            dve.wait_ge(s_lg, TILES)
            T5 = [P, TILES, NG]
            lg, le = logit[:, :, 0:NG], logit[:, :, NG:]
            rev = con[:, C_REV:C_REV + NG][:, None, :].to_broadcast(T5)

            def tt(out, a, b, op):
                link(v.tensor_tensor(out=out, in0=a, in1=b, op=op))

            def first_max(src, top, onehot):
                link(v.tensor_reduce(out=top, in_=src, axis=AX.X, op=ALU.max))
                tt(onehot, src, top.unsqueeze(2).to_broadcast(T5), ALU.is_equal)
                tt(onehot, onehot, rev, ALU.mult)
                link(v.tensor_reduce(out=rtmp, in_=onehot, axis=AX.X, op=ALU.max))
                tt(onehot, onehot, rtmp.unsqueeze(2).to_broadcast(T5), ALU.is_equal)

            first_max(lg, rtop, rgrp)
            v.tensor_tensor(out=gx[:, :, 0:NG], in0=lg, in1=rtop.unsqueeze(2).to_broadcast(T5),
                            op=ALU.subtract).then_inc(s_gin, 1)
            for e in range(EPG):
                tt(rsel, le.rearrange("p t (g e) -> p t g e", e=EPG)[:, :, :, e], rgrp, ALU.mult)
                link(v.tensor_reduce(out=rin[:, :, e], in_=rsel, axis=AX.X, op=ALU.add))
            first_max(rin, rm1, roh1)
            link(v.tensor_scalar(rsel, roh1, -3.0e38, None, ALU.mult))
            link(v.tensor_scalar(rin2, roh1, -1.0, 1.0, ALU.mult, ALU.add))
            tt(rin2, rin2, rin, ALU.mult)
            tt(rin2, rin2, rsel, ALU.add)
            first_max(rin2, rm2, roh2)
            v.tensor_tensor(out=gx[:, :, 4], in0=rm2, in1=rm1, op=ALU.subtract).then_inc(s_gin, 1)
            dve.wait_ge(s_gexp, 2)
            link(v.tensor_reduce(out=rtop, in_=gx[:, :, 0:NG], axis=AX.X, op=ALU.add))
            link(v.tensor_scalar(rtmp, gx[:, :, 4], 1.0, None, ALU.add))
            tt(rtmp, rtmp, rtop, ALU.mult)
            link(v.reciprocal(rm1, rtmp))
            tt(rm2, gx[:, :, 4], rm1, ALU.mult)
            tt(roh1, roh1, rm1.unsqueeze(2).to_broadcast(T5), ALU.mult)
            tt(roh2, roh2, rm2.unsqueeze(2).to_broadcast(T5), ALU.mult)
            tt(roh1, roh1, roh2, ALU.add)
            gv = gates[:].rearrange("p t (g e) -> p t g e", e=EPG)
            for gi in range(NG):
                last = v.tensor_tensor(out=gv[:, :, gi, :], in0=roh1,
                                       in1=rgrp[:, :, gi:gi + 1].to_broadcast([P, TILES, EPG]),
                                       op=ALU.mult)
            last.then_inc(s_gates, 1)
            dve.wait_ge(s_gates, 1)

            for i in range(NE * TILES + 1):
                if i < NE * TILES:
                    e, t = divmod(i, TILES)
                    n = rows(t)
                    dve.wait_ge(s_h1e, i + 1)
                    if i >= 2:
                        dve.wait_ge(s_hTp, i - 1)
                    v.scalar_tensor_tensor(out=hg[i % 2][0:n], in0=hb[i % 2][0:n],
                                           scalar=gates[0:n, t, e:e + 1],
                                           in1=bank[i % 2][0:n, FE:2 * FE], op0=ALU.mult,
                                           op1=ALU.mult).then_inc(s_h2, 1)
                if i:
                    e, t = divmod(i - 1, TILES)
                    n = rows(t)
                    dve.wait_ge(s_dn, i)
                    if e:
                        dve.wait_ge(s_y, i - TILES)
                    for c in range(2):
                        o = Y[0:n, t, c * 512:(c + 1) * 512]
                        src = bank[4 + 2 * ((i - 1) % 2) + c][0:n]
                        if e == 0:
                            last = v.tensor_copy(o, src)
                        else:
                            last = v.tensor_tensor(out=o, in0=o, in1=src, op=ALU.add)
                    last.then_inc(s_y, 1)
            for t in range(TILES):
                n = rows(t)
                dve.wait_ge(s_frms, t + 1)
                link(v.reciprocal(ss[0:n, 3, t, 0:1], ss[0:n, 3, t, 0:1]))
                if t == 0:
                    dve.wait_ge(s_g2, 16 * 9)
                link(v.scalar_tensor_tensor(
                    out=Y[0:n, t], in0=Y[0:n, t], scalar=ss[0:n, 3, t, 0:1],
                    in1=tab["g2" + tag(t)][0:n], op0=ALU.mult, op1=ALU.mult))
                v.tensor_tensor(out=x[0:n, t], in0=x[0:n, t], in1=Y[0:n, t], op=ALU.add)\
                    .then_inc(s_fin, 1)


_INS = ['x_prompt', 'x_sample', 'state_conv', 'state_lru', 'state_ret', 'c_prompt', 'c_sample',
        'w_mod', 'b_mod', 'norm_pre_mix', 'norm_post_mix', 'norm_pre_ffn', 'norm_post_ffn', 'w_in',
        'conv_w', 'conv_b', 'w_rgate', 'b_rgate', 'w_igate', 'b_igate', 'lru_lambda', 'ret_gn_w',
        'w_out', 'w_router_group', 'b_router_group', 'w_router_expert', 'b_router_expert',
        'w_exp_gate', 'w_exp_up', 'w_exp_down']
_OUTS = [(1, SEQ, D), (DB, DT, D), (1, 1, CONVW - 1, DL), (1, 1, DL), (1, 1, NH, DK, DK),
         (1, DB, CONVW - 1, DL), (1, DB, DL), (1, DB, NH, DK, DK)]


def kernel(**inputs):
    import concourse.bacc as _bacc
    from concourse.bass_utils import run_bass_kernel_spmd as _run

    nc = _bacc.Bacc("TRN2", target_bir_lowering=False, num_devices=1)
    arrays, args = {}, []
    for name in _INS:
        a = np.ascontiguousarray(inputs[name])
        arrays[f"in_{name}_dram"] = a
        args.append(nc.dram_tensor(f"in_{name}_dram", a.shape, F32, kind="ExternalInput").ap())
    arrays["in_consts_dram"] = shape_constants()
    args.append(nc.dram_tensor("in_consts_dram", (P, NCONST), F32, kind="ExternalInput").ap())
    for i, shape in enumerate(_OUTS):
        args.append(nc.dram_tensor(f"out_{i}_dram", shape, F32, kind="ExternalOutput").ap())
    build(nc, *args)
    r = _run(nc, [arrays], core_ids=[0])
    return tuple(r.results[0][f"out_{i}_dram"] for i in range(len(_OUTS)))
```

```python
import math
from contextlib import ExitStack

import numpy as np

import concourse.bass as bass
from concourse import mybir

ALU = mybir.AluOpType
ACT = mybir.ActivationFunctionType
AX = mybir.AxisListType
F32 = mybir.dt.float32
F16 = mybir.dt.float16
I32 = mybir.dt.int32
U32 = mybir.dt.uint32

P = 128
D = 1024
SEQ = 512
DB, DT = 8, 8
NS = DB * DT
NTOK = SEQ + NS
KT = D // P
DL = 512
MT = DL // P
CONVW = 4
NH = 4
DK = 128
PAST = 4096
NE = 16
NG = 4
EPG = 4
FE = 256
FT = FE // P
NORM_EPS = 1e-6
GN_EPS = 1e-5
TILES = SEQ // P + 1
SROWS = NS
XRW = 3 + SEQ + DB * (3 + DT)
NMOD = 3
SLOTS = 9
CAPACITY = P
AHEAD = 3
SLOT = 2048

LOG_G = [math.log1p(-(2.0 ** (-5.0 - h))) for h in range(NH)]
GAMMA_CHUNK = [math.exp(P * g) for g in LOG_G]
GAMMA_STEP = [math.exp(DT * g) for g in LOG_G]

C_ID = 0
C_MP = C_ID + P
C_MS = C_MP + P
C_COS = C_MS + NS
C_SIN = C_COS + TILES * 64
C_DQ = C_SIN + TILES * 64
C_DK = C_DQ + 2 * NH
C_BM = C_DK + 2 * NH
C_REV = C_BM + DB
C_TRI = C_REV + NG
C_IOTA = C_TRI + P
C_TOK = C_IOTA + P
C_VALID = C_TOK + TILES
C_BASE = C_VALID + TILES
NCONST = C_BASE + NE


def rows(t):
    return P if t < TILES - 1 else SROWS


def shape_constants():
    c = np.zeros((P, NCONST), np.float32)
    i = np.arange(P)
    c[:, C_ID:C_ID + P] = np.eye(P)
    c[:, C_MP:C_MP + P] = i[:, None] <= i[None, :]
    s = np.arange(NS)
    same = (s[:, None] // DT) == (s[None, :] // DT)
    c[:NS, C_MS:C_MS + NS] = same & (s[:, None] <= s[None, :])
    half = DK // 2
    inv = np.float32(10000.0) ** (-np.arange(half, dtype=np.float32) / np.float32(half))
    for t in range(TILES):
        pos = (t * P + i if t < TILES - 1 else PAST + i % DT).astype(np.float32)
        ang = (pos[:, None] * inv[None, :].astype(np.float32)).astype(np.float32)
        c[:, C_COS + t * 64:C_COS + (t + 1) * 64] = np.cos(ang.astype(np.float64))
        c[:, C_SIN + t * 64:C_SIN + (t + 1) * 64] = np.sin(ang.astype(np.float64))
    for h in range(NH):
        c[:, C_DQ + h] = np.exp((i + 1) * LOG_G[h]) * DK ** -0.5
        c[:, C_DQ + NH + h] = np.exp((i % DT + 1) * LOG_G[h]) * DK ** -0.5
        c[:, C_DK + h] = np.exp(-(i + 1) * LOG_G[h])
        c[:, C_DK + NH + h] = np.exp(-(i % DT + 1) * LOG_G[h])
    for b in range(DB):
        c[b * DT:(b + 1) * DT, C_BM + b] = 1.0
    c[:, C_REV:C_REV + NG] = NG - np.arange(NG)
    c[:, C_TRI:C_TRI + P] = i[:, None] < i[None, :]
    c[:, C_IOTA:C_IOTA + P] = 1 + i
    for t in range(TILES):
        c[:, C_TOK + t] = t * P + i
        c[:, C_VALID + t] = i < rows(t)
    c[:, C_BASE:C_BASE + NE] = P * np.arange(NE)
    return c


def weight_pieces():
    out = [("mod", 0, k) for k in range(KT)]
    out += [("in", 0, 0), ("in", 0, 1)] + [("mod", 1, k) for k in range(KT)]
    out += [("in", 1, 0), ("in", 1, 1)] + [("mod", 2, k) for k in range(KT)]
    out += [("in", c, h) for c in range(2, 6) for h in range(2)]
    out += [("out", n, h) for n in range(2) for h in range(2)]
    for e in range(NE):
        out += [("wg", e, 0), ("wu", e, 0), ("wd", e, 0)]
    return out


def used_up(piece):
    kind, a, b = piece
    if kind == "mod":
        return {0: 0, 1: 10, 2: 30}[a] + b
    if kind == "in":
        return {0: 15.5, 1: 35.5}.get(a, 50 + a)
    if kind == "out":
        return 60
    return 70 + a + (1.5 if kind == "wd" else 0)


def place_pieces():
    held = [(-1 + s * 0.01, None) for s in range(SLOTS)]
    uses = [0] * SLOTS
    slot, before, nth = {}, {}, {}
    for p in weight_pieces():
        s = min(range(SLOTS), key=lambda j: held[j][0])
        slot[p], before[p] = s, held[s][1]
        uses[s] += 1
        nth[p] = uses[s]
        held[s] = (used_up(p), p)
    return slot, before, nth


def build(nc, x_prompt, x_sample, state_conv, state_lru, state_ret, c_prompt, c_sample, w_mod, b_mod,
          norm_pre_mix, norm_post_mix, norm_pre_ffn, norm_post_ffn, w_in, conv_w, conv_b, w_rgate,
          b_rgate, w_igate, b_igate, lru_lambda, ret_gn_w, w_out, w_router_group, b_router_group,
          w_router_expert, b_router_expert, w_exp_gate, w_exp_up, w_exp_down, consts,
          y_prompt, y_sample, conv_prompt, lru_prompt, ret_prompt, conv_sample, lru_sample,
          ret_sample):
    slot, before, nth = place_pieces()
    with ExitStack() as ctx:
        def sb(name, shape, dt=F32):
            return ctx.enter_context(nc.sbuf_tensor(name, shape, dt))

        def sem(name):
            return ctx.enter_context(nc.semaphore(name))

        mod_rows_dram = nc.dram_tensor("mod_rows_dram", (1 + DB, 6 * D), F32, kind="Internal").ap()

        u2_dram = nc.dram_tensor("u2_dram", (NTOK, D), F32, kind="Internal").ap()
        slots_dram = nc.dram_tensor("slots_dram", (NE * P, D), F32, kind="Internal").ap()

        bank = [ctx.enter_context(nc.psum_tensor(f"bank{i}", [P, 512], F32)) for i in range(8)]

        x = sb("x", [P, TILES, D])
        uT = sb("uT", [P, KT, NTOK])
        ring = sb("ring", [P, SLOTS, SLOT])
        hy = sb("hy", [P, MT, NTOK])
        outbT = sb("outbT", [P, NH, NTOK])
        rowsT = sb("rowsT", [P, 416])
        con = sb("con", [P, NCONST])
        modT = sb("modT", [P, 4, 4, 32])
        wgate = sb("wgate", [P, 2, MT, 64])
        gnw = sb("gnw", [P, DL])
        wrt = sb("wrt", [P, KT, NG + NE])
        brt = sb("brt", [P, NG + NE])
        ss = sb("ss", [P, 4, TILES, 2])
        softp = sb("softp", [P, 8, MT])
        gst = sb("gst", [P, NH, 6])
        gmv = sb("gmv", [P, NH, 2])
        grs = sb("grs", [P, NH])
        tails = sb("tails", [P, MT, 36])
        logit = sb("logit", [P, TILES, NG + NE])
        gates = sb("gates", [P, TILES, NE])
        tri = sb("tri", [P, P], F16)
        ones = sb("ones", [P, P], F16)
        tok = sb("tok", [P, TILES], F16)
        sel = sb("sel", [P, TILES, NE], F16)
        over = sb("over", [P, 1], I32)
        slot_tok = sb("slot_tok", [P, NE], U32)
        tok_slot = sb("tok_slot", [P, 2, TILES], U32)
        tailrow = sb("tailrow", [36, DL])
        rtb = sb("rtb", [P, 168])
        eps = sb("eps", [P, 2])
        arena = sb("arena", [P, 14336])

        def region(at, *dims):
            v = arena[:, at:at + int(np.prod(dims))]
            if len(dims) == 2:
                v = v.rearrange("p (a b) -> p a b", b=dims[1])
            return v

        xn = region(0, TILES, D)
        bm = region(5120, NMOD, 512)
        nm = region(6656, NMOD, 512)
        crow = hy[0:32, 0:2, :].rearrange("p a b -> p (a b)")[:, 0:D]
        par = hy[0:8, 2, 0:DL]
        srow = hy[0:32, 3, 0:DL]
        xr = [region(8192 + i * XRW, XRW) for i in range(2)]
        xc = [region(9408 + i * NTOK, NTOK) for i in range(2)]
        ge = [region(10560 + i * NTOK, NTOK) for i in range(2)]
        R, I, Q = (region(11712 + i * NTOK, NTOK) for i in range(3))
        A = region(13440, NTOK)
        Z = ge[1]
        qs, ks, tB, tS, kr1, vv1, gg1, kr0, vv0, gg0, qr, S, qT, kT, sm, ob = (
            region(i * 512, 512) for i in range(16))
        kr, vv, gg = [kr0, kr1], [vv0, vv1], [gg0, gg1]
        s0 = [region(0, DB, DK), region(1024, DB, DK)]
        vblk = region(2048, DB, DK)
        tab = {n: region(8192 + i * D, D)
               for i, n in enumerate(("g1p", "g1s", "a2p", "a2s", "s2p", "s2s"))}
        tab["g2p"], tab["g2s"] = tab["a2p"], tab["a2s"]
        t1 = region(3072, D)
        u2 = [region(4096, D), region(5120, D)]
        junk = region(6144, D)
        Y = region(0, TILES, D)
        hb = [region(5120 + i * FE, FE) for i in range(2)]
        hg = [region(5632 + i * FE, FE) for i in range(2)]
        hT = [region(6144 + i * FE, FE) for i in range(2)]
        xg = [region(i * D, D) for i in range(2)]
        xgT = [region(2048 + i * D, KT, P) for i in range(2)]
        eo = [region(6656 + i * D, D) for i in range(2)]
        hit = [arena[:, 8704 + i * 320:8704 + (i + 1) * 320].bitcast(F16)
               .rearrange("p (t s) -> p t s", s=P) for i in range(2)]
        og = [[region(5120 + (2 * i + k) * D, D) for k in range(2)] for i in range(2)]
        yj = region(9216, D)

        gx = rtb[:, 0:25].rearrange("p (t g) -> p t g", g=5)
        rtop, rtmp, rm1, rm2 = (rtb[:, 25 + 5 * i:30 + 5 * i] for i in range(4))
        rgrp, rsel, rin, rin2, roh1, roh2 = (
            rtb[:, 48 + 20 * i:68 + 20 * i].rearrange("p (t g) -> p t g", g=NG) for i in range(6))
        oh = [region(13200 + i * TILES * NE, TILES, NE) for i in range(2)]
        rank, rank1, place = (region(13200 + i * TILES * NE, TILES, NE) for i in range(2, 5))
        count1 = region(13600, 1)
        gcol = region(13640, TILES, 1)
        slotf = region(13616, TILES)

        ident = con[:, C_ID:C_ID + P]
        cosv = con[:, C_COS:C_COS + TILES * 64].rearrange("p (t d) -> p t d", d=64)
        sinv = con[:, C_SIN:C_SIN + TILES * 64].rearrange("p (t d) -> p t d", d=64)
        cT = rowsT[:, 0:256].rearrange("p (k r) -> p k r", r=32)
        parT = rowsT[:, 256:288].rearrange("p (m r) -> p m r", r=8)
        stT = rowsT[:, 288:416].rearrange("p (m r) -> p m r", r=32)

        s_c = sem("s_c")
        s_zero = sem("s_zero")
        s_x = sem("s_x")
        s_con = sem("s_con")
        s_par = sem("s_par")
        s_bm = sem("s_bm")
        s_wg = sem("s_wg")
        s_misc = sem("s_misc")
        landed = [sem(f"landed{i}") for i in range(SLOTS)]
        s_silu = sem("s_silu")
        s_sq = sem("s_sq")
        s_xn = sem("s_xn")
        s_setupT = sem("s_setupT")
        s_rowsT = sem("s_rowsT")
        s_uTp = sem("s_uTp")
        s_mod = sem("s_mod")
        s_modrow = sem("s_modrow")
        s_modTp = sem("s_modTp")
        s_modT = sem("s_modT")
        s_uTa = sem("s_uTa")
        s_uTd = sem("s_uTd")
        s_xr = sem("s_xr")
        s_xre = sem("s_xre")
        s_yge = sem("s_yge")
        s_conv = sem("s_conv")
        s_gate = sem("s_gate")
        s_sig = sem("s_sig")
        s_spin = sem("s_spin")
        s_spout = sem("s_spout")
        s_spexp = sem("s_spexp")
        s_spln = sem("s_spln")
        s_tanh = sem("s_tanh")
        s_ix = sem("s_ix")
        s_lru = sem("s_lru")
        s_h = sem("s_h")
        s_hy = sem("s_hy")
        s_tailT = sem("s_tailT")
        s_tail = sem("s_tail")
        s_proj = sem("s_proj")
        s_pe = sem("s_pe")
        s_rot = sem("s_rot")
        s_qkT = sem("s_qkT")
        s_qkTe = sem("s_qkTe")
        s_sc = sem("s_sc")
        s_sm = sem("s_sm")
        s_o = sem("s_o")
        s_kv = sem("s_kv")
        s_st = sem("s_st")
        s_oT = sem("s_oT")
        s_oTe = sem("s_oTe")
        s_oTT = sem("s_oTT")
        s_gg = sem("s_gg")
        s_ob = sem("s_ob")
        s_obT = sem("s_obT")
        s_obTe = sem("s_obTe")
        s_s0 = [sem("s_s0a"), sem("s_s0b")]
        s_vblk = sem("s_vblk")
        s_cross = sem("s_cross")
        s_skv = sem("s_skv")
        s_snew = sem("s_snew")
        s_modst = sem("s_modst")
        s_tab = sem("s_tab")
        s_out = sem("s_out")
        s_msq = sem("s_msq")
        s_x1 = sem("s_x1")
        s_xsq = sem("s_xsq")
        s_u2 = sem("s_u2")
        s_u2T = sem("s_u2T")
        s_u2Te = sem("s_u2Te")
        s_rtr = sem("s_rtr")
        s_lg = sem("s_lg")
        s_gexp = sem("s_gexp")
        s_gin = sem("s_gin")
        s_gates = sem("s_gates")
        s_u2st = [sem("s_u2st0"), sem("s_u2st1")]
        s_half = sem("s_half")
        s_rsel = sem("s_rsel")
        s_rank = sem("s_rank")
        s_over = sem("s_over")
        s_hit = sem("s_hit")
        s_tokn = sem("s_tokn")
        s_idx = sem("s_idx")
        s_xg = [sem("s_xg0"), sem("s_xg1")]
        s_xgT = sem("s_xgT")
        s_xgTa = sem("s_xgTa")
        s_xgTd = sem("s_xgTd")
        s_in = sem("s_in")
        s_hs = sem("s_hs")
        s_hm = sem("s_hm")
        s_ht = sem("s_ht")
        s_hte = sem("s_hte")
        s_down = sem("s_down")
        s_eoa = sem("s_eoa")
        s_eod = sem("s_eod")
        s_ost = [sem("s_ost0"), sem("s_ost1")]
        s_place = sem("s_place")
        s_og = [sem("s_og0"), sem("s_og1")]
        s_f = sem("s_f")
        s_fw = sem("s_fw")
        s_h1 = sem("s_h1")
        s_h1e = sem("s_h1e")
        s_h2 = sem("s_h2")
        s_hTp = sem("s_hTp")
        s_hTe = sem("s_hTe")
        s_dn = sem("s_dn")
        s_y = sem("s_y")
        s_fsq = sem("s_fsq")
        s_g2 = sem("s_g2")
        s_fin = sem("s_fin")
        s_store = sem("s_store")
        s_ssto = sem("s_ssto")
        s_yout = sem("s_yout")
        s_tl = sem("s_tl")
        s_fb = sem("s_fb")
        s_sp = sem("s_sp")
        s_hit0 = sem("s_hit0")
        s_gcol = sem("s_gcol")
        s_xrms = sem("s_xrms")
        s_root = sem("s_root")
        s_var = sem("s_var")
        s_dev = sem("s_dev")
        s_msum = sem("s_msum")
        s_mrms = sem("s_mrms")
        s_x1rms = sem("s_x1rms")
        s_frms = sem("s_frms")
        s_vec = sem("s_vec")
        s_act = sem("s_act")
        s_pool = sem("s_pool")

        used = {}
        for p in weight_pieces():
            kind, a, b = p
            if kind == "mod":
                used[p] = (s_mod, KT * a + b + 1)
            elif kind == "in":
                used[p] = (s_xr, MT * (a + 1)) if a < 2 else (s_proj, 4 * (TILES - 1) + a - 1)
            elif kind == "out":
                used[p] = (s_out, TILES)
            elif kind in ("wg", "wu"):
                used[p] = (s_in, a + 1)
            else:
                used[p] = (s_down, a + 1)
        expert_pieces = [p for p in weight_pieces() if p[0] in ("wg", "wu", "wd")]
        early = [p for p in expert_pieces if before[p][0] not in ("wg", "wu", "wd")]
        late = expert_pieces[len(early):]
        assert early == expert_pieces[:SLOTS]

        def weights(eng, piece):
            eng.wait_ge(landed[slot[piece]], 16 * nth[piece])
            return ring[:, slot[piece], :]

        def spread(eng, parts, done):
            for name, k in parts:
                eng.dma_start(tab[name + "p"], mod_rows_dram[0:1, k * D:(k + 1) * D]
                              .to_broadcast([P, D])).then_inc(done, 16)
                for b in range(DB):
                    eng.dma_start(tab[name + "s"][b * DT:(b + 1) * DT, :],
                                  mod_rows_dram[1 + b:2 + b, k * D:(k + 1) * D]
                                  .to_broadcast([DT, D])).then_inc(done, 16)

        block = ctx.enter_context(nc.Block())

        def overflow(eng):
            eng.wait_ge(s_over, 1)
            return eng.value_load(over[0:1, 0:1], min_val=0, max_val=1) > 0

        @block.sync
        def _(sp):
            def load(p):
                kind, a, b = p
                if before[p] is not None:
                    sp.wait_ge(*used[before[p]])
                dst = ring[:, slot[p], :]
                if kind == "mod":
                    src = w_mod[0, b * P:(b + 1) * P, a * 2048:(a + 1) * 2048]
                elif kind in ("in", "out"):
                    w = w_in if kind == "in" else w_out
                    src = w[0, b * 4 * P:(b + 1) * 4 * P, a * 512:(a + 1) * 512].rearrange(
                        "(k p) n -> p k n", p=P)
                    dst = dst.rearrange("p (k n) -> p k n", n=512)
                elif kind == "wd":
                    src = w_exp_down[0, a].rearrange("(k p) n -> p k n", p=P)
                    dst = dst.rearrange("p (k n) -> p k n", n=D)
                else:
                    w = w_exp_gate if kind == "wg" else w_exp_up
                    src = w[0, a].rearrange("(k p) n -> p k n", p=P)
                    dst = dst.rearrange("p (k n) -> p k n", n=FE)
                sp.dma_start(dst, src).then_inc(landed[slot[p]], 16)

            sp.wait_ge(s_zero, 1)
            sp.dma_start(crow[0:1, :], c_prompt).then_inc(s_c, 16)
            sp.dma_start(crow[1:1 + DB, :], c_sample).then_inc(s_c, 16)
            for r in range(CONVW):
                sp.dma_start(par[r:r + 1, :], conv_w[0, r:r + 1, :]).then_inc(s_par, 16)
            sp.dma_start(par[4:5, :], conv_b).then_inc(s_par, 16)
            sp.dma_start(par[5:6, :], b_rgate.rearrange("a n k -> a (n k)")).then_inc(s_par, 16)
            sp.dma_start(par[6:7, :], b_igate.rearrange("a n k -> a (n k)")).then_inc(s_par, 16)
            sp.dma_start(par[7:8, :], lru_lambda).then_inc(s_par, 16)
            sp.dma_start(srow[0:24, :], state_conv.rearrange("a b w c -> (a b w) c"))\
                .then_inc(s_par, 16)
            sp.dma_start(srow[24:32, :], state_lru[0]).then_inc(s_par, 16)
            for p in weight_pieces():
                if p not in late:
                    load(p)
            with sp.If(overflow(sp)):
                for p in early:
                    sp.wait_ge(landed[slot[p]], 16 * nth[p])
                with sp.Fori(0, NE) as e:
                    sp.wait_ge(s_y, e * TILES + 1)
                    for j, (w, n) in enumerate(((w_exp_gate, FE), (w_exp_up, FE), (w_exp_down, D))):
                        sp.dma_start(ring[:, j, :].rearrange("p (k n) -> p k n", n=n),
                                     w[0, bass.ds(e, 1)].rearrange("a (k p) n -> p (a k) n", p=P))\
                            .then_inc(s_fw, 16)
            with sp.Else():
                for p in late:
                    load(p)

        @block.gpsimd
        def _(pool):
            pool.memset(hy[0:32, 0:2, :], 0.0).then_inc(s_zero, 1)
            pool.memset(ss[:], 1.0).then_inc(s_zero, 1)
            pool.memset(eps[:, 0:1], NORM_EPS).then_inc(s_zero, 1)
            pool.memset(eps[:, 1:2], GN_EPS).then_inc(s_zero, 1)
            for i in range(2):
                pool.memset(xr[i][:, 0:3], 0.0).then_inc(s_zero, 1)
            pool.wait_ge(s_zero, 6)
            pool.memset(nm[0:64, 0, :], 1.0).then_inc(s_zero, 1)
            pool.wait_ge(s_zero, 7)
            pool.memset(nm[64:128, 1, :], 1.0).then_inc(s_zero, 1)

            for j in range(4):
                pool.dma_start(bm[32 * j:32 * j + 32, :, :],
                               b_mod.rearrange("a (g j n) -> a g j n", g=NMOD, j=4)[:, :, j, :]
                               .to_broadcast([32, NMOD, 512])).then_inc(s_bm, 16)
            for gq, j0, w in ((0, 2, norm_pre_mix), (1, 0, norm_post_mix), (2, 0, norm_pre_ffn),
                              (2, 2, norm_post_ffn)):
                for j in range(2):
                    q0 = 32 * (j0 + j)
                    pool.dma_start(nm[q0:q0 + 32, gq, :], w[0:1, j * 512:(j + 1) * 512]
                                   .to_broadcast([32, 512])).then_inc(s_bm, 16)
            for gi, w in enumerate((w_rgate, w_igate)):
                wv = w[0].rearrange("(m a) j k -> a j m k", a=2)
                for a in range(2):
                    pool.dma_start(wgate[64 * a:64 * a + 64, gi, :, :], wv[a]).then_inc(s_wg, 16)
            pool.dma_start(gnw[:], ret_gn_w.to_broadcast([P, DL])).then_inc(s_misc, 16)
            pool.dma_start(wrt[:, :, 0:NG], w_router_group[0].rearrange("(k p) n -> p k n", p=P))\
                .then_inc(s_misc, 16)
            pool.dma_start(wrt[:, :, NG:], w_router_expert[0].rearrange("(k p) n -> p k n", p=P))\
                .then_inc(s_misc, 16)
            pool.dma_start(brt[:, 0:NG], b_router_group.to_broadcast([P, NG])).then_inc(s_misc, 16)
            pool.dma_start(brt[:, NG:], b_router_expert.to_broadcast([P, NE])).then_inc(s_misc, 16)

            for gq in (1, 2):
                pool.wait_ge(s_modrow, gq + 1)
                for j in range(4):
                    c0 = gq * 2048 + j * 512
                    pool.dma_start(mod_rows_dram[:, c0:c0 + 512], bm[32 * j:32 * j + 1 + DB, gq, :])\
                        .then_inc(s_modst, 16)
            pool.wait_ge(s_modst, 16 * 8)
            pool.wait_ge(s_hy, MT)
            spread(pool, (("g1", 2), ("s2", 3), ("a2", 4)), s_tab)

            pool.wait_ge(s_tail, 1)
            tl = tailrow
            pool.dma_start(conv_prompt.rearrange("a b w c -> (a b w) c"), tl[0:3, :])\
                .then_inc(s_store, 16)
            pool.dma_start(conv_sample.rearrange("a b w c -> (a b w) c"), tl[3:27, :])\
                .then_inc(s_store, 16)
            pool.dma_start(lru_prompt[0], tl[27:28, :]).then_inc(s_store, 16)
            pool.dma_start(lru_sample[0], tl[28:36, :]).then_inc(s_store, 16)
            pool.wait_ge(s_st, TILES - 1)
            pool.dma_start(ret_prompt[0, 0].rearrange("h k e -> k h e"),
                           S.rearrange("p (h e) -> p h e", e=DK)).then_inc(s_store, 16)
            for h in range(NH):
                if h == 0:
                    pool.wait_ge(s_rot, 2 * TILES)
                    pool.wait_ge(s_st, TILES - 1)
                if h >= 2:
                    pool.wait_ge(s_ssto, 16 * (h - 1))
                pool.dma_start(s0[h % 2], state_ret[0, :, h].rearrange("b k e -> k b e"))\
                    .then_inc(s_s0[h % 2], 16)
                pool.wait_ge(s_pe, 4 * TILES)
                if h == 0:
                    pool.wait_ge(s_kv, TILES - 1)
                if h > 0:
                    pool.wait_ge(s_skv, 2 * h)
                pool.tensor_tensor(
                    out=vblk[0:NS], in0=vv[0][0:NS, None, h * DK:(h + 1) * DK].to_broadcast([NS, DB, DK]),
                    in1=con[0:NS, C_BM:C_BM + DB].unsqueeze(2).to_broadcast([NS, DB, DK]),
                    op=ALU.mult).then_inc(s_vblk, 1)
                if h >= 1:
                    pool.wait_ge(s_snew, 2 * h)
                    pool.dma_start(ret_sample[0, :, h - 1].rearrange("b k e -> k b e"),
                                   s0[(h - 1) % 2]).then_inc(s_ssto, 16)
            pool.wait_ge(s_snew, 2 * NH)
            pool.dma_start(ret_sample[0, :, NH - 1].rearrange("b k e -> k b e"),
                           s0[(NH - 1) % 2]).then_inc(s_ssto, 16)
            pool.wait_ge(s_u2, TILES)
            spread(pool, (("g2", 5),), s_g2)
            for k in range(2):
                pool.wait_ge(s_u2st[k], 16 * ((TILES + 1 - k) // 2))
            with pool.If(overflow(pool)):
                pool.nop()
            with pool.Else():
                for e in range(NE):
                    pool.wait_ge(s_idx, e + 1)
                    if e >= 2:
                        pool.wait_ge(s_xgT, e - 1)
                    pool.indirect_dma_start(
                        out=xg[e % 2], out_offset=None, in_=u2_dram,
                        in_offset=bass.IndirectOffsetOnAxis(ap=slot_tok[:, e:e + 1], axis=0))\
                        .then_inc(s_xg[e % 2], 16)
                pool.wait_ge(s_place, 1)
                for k in range(2):
                    pool.wait_ge(s_ost[k], 16 * NE // 2)
                for t in range(TILES):
                    n = rows(t)
                    if t >= 2:
                        pool.wait_ge(s_f, t - 1)
                    for k in range(2):
                        pool.indirect_dma_start(
                            out=og[t % 2][k][0:n], out_offset=None, in_=slots_dram,
                            in_offset=bass.IndirectOffsetOnAxis(ap=tok_slot[0:n, k, t:t + 1],
                                                                axis=0))\
                            .then_inc(s_og[t % 2], 16)
            pool.wait_ge(s_store, 16 * 5)
            pool.wait_ge(s_ssto, 16 * NH)


        @block.tensor
        def _(pe):
            def mm(out, lhsT, rhs, first, last):
                return nc.tensor.matmul(out, lhsT, rhs, start=first, stop=last)

            def turn(out, src):
                return nc.tensor.transpose(out, src, ident[0:src.shape[0], 0:src.shape[0]])

            pe.wait_ge(s_con, 16)
            pe.wait_ge(s_silu, 1)
            pe.wait_ge(s_par, 16 * 10)
            for k in range(KT):
                turn(bank[0][:, 32 * k:32 * k + 32], crow[:, k * P:(k + 1) * P])
            for m in range(MT):
                turn(bank[0][:, 256 + 8 * m:264 + 8 * m], par[:, m * P:(m + 1) * P])
            for m in range(MT):
                last = turn(bank[0][:, 288 + 32 * m:320 + 32 * m], srow[:, m * P:(m + 1) * P])
            last.then_inc(s_setupT, 1)

            def turn_x(k, b):
                for t in range(TILES - 1):
                    last = turn(bank[b][:, t * P:(t + 1) * P], xn[:, t, k * P:(k + 1) * P])
                last.then_inc(s_uTp, 1)

            pe.wait_ge(s_xn, TILES)
            for k in range(7):
                turn_x(k, k + 1)

            def mod_step(gq, k, b):
                w = weights(pe, ("mod", gq, k))
                for j in range(4):
                    last = mm(bank[b][32 * j:32 * j + 32, :], cT[:, k, :],
                              w[:, j * 512:(j + 1) * 512], k == 0, k == KT - 1)
                last.then_inc(s_mod, 1)

            pe.wait_ge(s_rowsT, 1)
            for k in range(KT):
                mod_step(0, k, 0)
            pe.wait_ge(s_modrow, 1)
            for q in range(4):
                last = turn(bank[0][:, q * P:(q + 1) * P], bm[:, 0, q * P:(q + 1) * P])
            last.then_inc(s_modTp, 1)
            pe.wait_ge(s_uTa, 1)
            turn_x(7, 1)
            pe.wait_ge(s_uTd, 1)
            for k in range(KT):
                last = nc.tensor.transpose(bank[2][:, k * NS:(k + 1) * NS],
                                           xn[0:NS, TILES - 1, k * P:(k + 1) * P], ident[0:NS, 0:NS])
            last.then_inc(s_uTp, 1)

            half = NTOK // 2

            def by_channel(c, m):
                i = MT * c + m
                w = [weights(pe, ("in", c, h)).rearrange("p (k n) -> p k n", n=512) for h in range(2)]
                if i == 0:
                    pe.wait_ge(s_uTa, 4)
                    pe.wait_ge(s_uTd, 5)
                if i >= 2:
                    if i - 2 < MT:
                        pe.wait_ge(s_xre, i - 1)
                    else:
                        pe.wait_ge(s_yge, i - 1 - MT)
                for n in range(2):
                    for k in range(KT):
                        last = mm(bank[2 * (i % 2) + n][:, 0:half],
                                  w[k // 4][:, k % 4, m * P:(m + 1) * P],
                                  uT[:, k, n * half:(n + 1) * half], k == 0, k == KT - 1)
                last.then_inc(s_xr, 1)

            def gate_products(m):
                pe.wait_ge(s_conv, m + 1)
                pe.wait_ge(s_wg, 16 * 4)
                if m >= 1:
                    pe.wait_ge(s_sig, 2 * m)
                for gi in range(2):
                    for a in range(2):
                        q = slice(64 * a, 64 * a + 64)
                        mm(bank[5 + gi][q, :], wgate[q, gi, m, :], xc[m % 2][q, 0:SEQ], True, True)
                    for a in range(2):
                        q = slice(64 * a, 64 * a + 64)
                        last = mm(bank[7][q, gi * NS:(gi + 1) * NS], wgate[q, gi, m, :],
                                  xc[m % 2][q, SEQ:NTOK], True, True)
                last.then_inc(s_gate, 1)

            by_channel(0, 0)
            mod_step(1, 0, 4)
            mod_step(1, 1, 4)
            by_channel(0, 1)
            mod_step(1, 2, 4)
            mod_step(1, 3, 4)
            gate_products(0)
            by_channel(0, 2)
            mod_step(1, 4, 4)
            mod_step(1, 5, 4)
            gate_products(1)
            by_channel(0, 3)
            mod_step(1, 6, 4)
            mod_step(1, 7, 4)
            gate_products(2)
            by_channel(1, 0)
            pe.wait_ge(s_modrow, 2)
            mod_step(2, 0, 4)
            mod_step(2, 1, 4)
            gate_products(3)
            for m in range(1, MT):
                by_channel(1, m)
                mod_step(2, 2 * m, 4)
                mod_step(2, 2 * m + 1, 4)
            pe.wait_ge(s_h, MT)
            pe.wait_ge(s_sig, 2 * MT)
            for m in range(MT):
                last = turn(bank[7][0:36, m * P:(m + 1) * P], tails[:, m, :])
            last.then_inc(s_tailT, 1)

            def project(t, c):
                w = [weights(pe, ("in", 2 + c, h)).rearrange("p (k n) -> p k n", n=512)
                     for h in range(2)]
                n = rows(t)
                if t == 0:
                    pe.wait_ge(s_yge, 3 + (c >= 2))
                else:
                    pe.wait_ge(s_pe, 4 * (t - 1) + c + 1)
                for k in range(KT):
                    last = mm(bank[c][0:n, :], uT[:, k, t * P:t * P + n], w[k // 4][:, k % 4, :],
                              k == 0, k == KT - 1)
                last.then_inc(s_proj, 1)

            def turn_qk(t):
                n = rows(t)
                pe.wait_ge(s_rot, 2 * t + 2)
                if t == 0:
                    pe.wait_ge(s_modrow, 3)
                    pe.wait_ge(s_sig, 2 * MT)
                else:
                    pe.wait_ge(s_obTe, t)
                    pe.wait_ge(s_st, t)
                for b, src in ((4, qr), (5, kr[t % 2])):
                    for h in range(NH):
                        last = turn(bank[b][:, h * P:h * P + n], src[0:n, h * P:(h + 1) * P])
                last.then_inc(s_qkT, 1)

            def scores(t):
                n = rows(t)
                pe.wait_ge(s_qkTe, t + 1)
                if t >= 1:
                    pe.wait_ge(s_sm, t)
                for h in range(NH):
                    last = mm(bank[6][0:n, h * n:(h + 1) * n], kT[:, h * P:h * P + n],
                              qT[:, h * P:h * P + n], True, True)
                last.then_inc(s_sc, 1)

            def outputs(t):
                pe.wait_ge(s_sm, t + 1)
                pe.wait_ge(s_pe, 4 * t + 3)
                if t == 0:
                    pe.wait_ge(s_tail, 1)
                else:
                    pe.wait_ge(s_ob, t)
                    pe.wait_ge(s_st, t)
                for h in range(NH):
                    c = slice(h * P, (h + 1) * P)
                    last = mm(bank[7][:, c], sm[:, c], vv[t % 2][:, c], True, t == 0)
                    if t:
                        last = mm(bank[7][:, c], qT[:, c], S[:, c], False, True)
                last.then_inc(s_o, 1)
                for h in range(NH):
                    c = slice(h * P, (h + 1) * P)
                    last = mm(bank[5][:, c], kr[t % 2][:, c], vv[t % 2][:, c], True, True)
                last.then_inc(s_kv, 1)

            def turn_out(t):
                n = rows(t)
                pe.wait_ge(s_ob, t + 1)
                for h in range(NH):
                    last = turn(bank[4][:, h * P:h * P + n], ob[0:n, h * P:(h + 1) * P])
                last.then_inc(s_obT, 1)

            def sample_outputs():
                t = TILES - 1
                pe.wait_ge(s_sm, t + 1)
                pe.wait_ge(s_pe, 4 * t + 3)
                pe.wait_ge(s_ob, t)
                for h in range(NH):
                    c = slice(h * DK, (h + 1) * DK)
                    o = bank[7][:, h * NS:(h + 1) * NS]
                    pe.wait_ge(s_s0[h % 2], 16 * (h // 2 + 1))
                    mm(o, vv[0][0:NS, c], sm[0:NS, h * NS:(h + 1) * NS], True, False)
                    for b in range(DB):
                        q0 = h * P + b * DT
                        last = mm(o[:, b * DT:(b + 1) * DT], s0[h % 2][:, b, :], qT[:, q0:q0 + DT],
                                  False, b == DB - 1)
                    last.then_inc(s_cross, 1)
                    pe.wait_ge(s_vblk, h + 1)
                    for n in range(2):
                        i = 2 * h + n
                        if i >= 2:
                            pe.wait_ge(s_snew, i - 1)
                        elif i == 0:
                            pe.wait_ge(s_obTe, t)
                        mm(bank[4 + n][:], kr[0][0:NS, c],
                           vblk[0:NS, 4 * n:4 * n + 4, :].rearrange("p b e -> p (b e)"),
                           True, True).then_inc(s_skv, 1)
                pe.wait_ge(s_oTe, 1)
                for h in range(NH):
                    last = turn(bank[6][0:NS, h * P:(h + 1) * P], sm[:, h * NS:(h + 1) * NS])
                last.then_inc(s_o, 1)

            for t in range(TILES + 1):
                steps = [lambda: turn_qk(t - 1), lambda: scores(t - 1), lambda: outputs(t - 1),
                         lambda: turn_out(t - 1)]
                if t == TILES:
                    steps[2] = sample_outputs
                for c in range(4):
                    if t < TILES:
                        project(t, c)
                    if t == TILES and c == 3:
                        pe.wait_ge(s_snew, 2 * NH)
                    if t:
                        steps[c]()

            def out_proj(t):
                n = rows(t)
                if t == 0:
                    pe.wait_ge(s_pe, 4 * TILES)
                    pe.wait_ge(s_obTe, TILES)
                if t >= 2:
                    pe.wait_ge(s_x1, t - 1)
                for c in range(2):
                    for k in range(KT):
                        w = weights(pe, ("out", c, k // 4)).rearrange("p (k n) -> p k n", n=512)
                        src = hy[:, k] if k < MT else outbT[:, k - MT]
                        last = mm(bank[2 * (t % 2) + c][0:n, :], src[:, t * P:t * P + n],
                                  w[:, k % 4, :], k == 0, k == KT - 1)
                last.then_inc(s_out, 1)

            def turn_u2(t):
                n = rows(t)
                pe.wait_ge(s_u2, t + 1)
                if t == 0:
                    pe.wait_ge(s_snew, 2 * NH)
                else:
                    pe.wait_ge(s_u2Te, 2 * t)
                for hf in range(2):
                    for k in range(4):
                        last = turn(bank[4 + hf][:, k * P:k * P + n],
                                    u2[t % 2][0:n, (4 * hf + k) * P:(4 * hf + k + 1) * P])
                    last.then_inc(s_u2T, 1)
                pe.wait_ge(s_u2Te, 2 * t + 2)
                pe.wait_ge(s_misc, 16 * 5)
                if t == 0:
                    pe.wait_ge(s_ob, TILES)
                else:
                    pe.wait_ge(s_lg, t)
                for k in range(KT):
                    last = mm(bank[6][0:n, 0:NG + NE], uT[:, k, t * P:t * P + n], wrt[:, k, :],
                              k == 0, k == KT - 1)
                last.then_inc(s_rtr, 1)

            for t in range(TILES + 1):
                if t < TILES:
                    out_proj(t)
                if t:
                    turn_u2(t - 1)

            pe.wait_ge(s_rsel, 1)
            pe.wait_ge(s_half, 3)
            pe.wait_ge(s_x1, TILES)
            pe.wait_ge(s_u2Te, 2 * TILES)
            pe.wait_ge(s_lg, TILES)
            for t in range(TILES):
                for j in range(t + 1):
                    mm(bank[7][:, t * NE:(t + 1) * NE], tri[:] if j == t else ones[:], sel[:, j],
                       j == 0, j == t)
            for j in range(TILES):
                last = mm(bank[7][:, TILES * NE:(TILES + 1) * NE], ones[:], sel[:, j], j == 0,
                          j == TILES - 1)
            last.then_inc(s_rank, 1)

            with pe.If(overflow(pe)):
                wg = ring[:, 0, :].rearrange("p (k n) -> p k n", n=FE)
                wu = ring[:, 1, :].rearrange("p (k n) -> p k n", n=FE)
                wd = ring[:, 2, :].rearrange("p (k n) -> p k n", n=D)
                with pe.Fori(0, NE) as e:
                    pe.wait_ge(s_fw, (e + 1) * 48)
                    for t in range(TILES):
                        n = rows(t)
                        pe.wait_ge(s_h2, e * TILES + t + 1)
                        for j, w in enumerate((wg, wu)):
                            for k in range(KT):
                                last = mm(bank[0][0:n, j * FE:(j + 1) * FE],
                                          uT[:, k, t * P:t * P + n], w[:, k, :], k == 0,
                                          k == KT - 1)
                        last.then_inc(s_h1, 1)
                        pe.wait_ge(s_h2, e * TILES + t + 2)
                        for k in range(FT):
                            last = turn(bank[2][:, k * P:(k + 1) * P],
                                        hg[0][:, k * P:(k + 1) * P])
                        last.then_inc(s_hTp, 1)
                        pe.wait_ge(s_hTe, e * TILES + t + 1)
                        pe.wait_ge(s_y, e * TILES + t + 1)
                        for c in range(2):
                            for k in range(FT):
                                last = mm(bank[4 + c][0:n, :], hT[0][:, k * P:k * P + n],
                                          wd[:, k, c * 512:(c + 1) * 512], k == 0, k == FT - 1)
                        last.then_inc(s_dn, 1)
            with pe.Else():
                def slot_tokens(e):
                    pe.wait_ge(s_hit, e + 1)
                    if e >= 1:
                        pe.wait_ge(s_idx, e)
                    for t in range(TILES):
                        last = mm(bank[7][:, 128:129], hit[e % 2][:, t, :], tok[:, t:t + 1],
                                  t == 0, t == TILES - 1)
                    last.then_inc(s_tokn, 1)

                def turn_input(e):
                    pe.wait_ge(s_xg[e % 2], 16 * (e // 2 + 1))
                    if e >= 1:
                        pe.wait_ge(s_xgTa, e)
                        pe.wait_ge(s_xgTd, e)
                    for k in range(KT):
                        last = turn(bank[2 + k // 4][:, (k % 4) * P:(k % 4 + 1) * P],
                                    xg[e % 2][:, k * P:(k + 1) * P])
                    last.then_inc(s_xgT, 1)

                def expert_in(e):
                    wg = weights(pe, ("wg", e, 0)).rearrange("p (k n) -> p k n", n=FE)
                    wu = weights(pe, ("wu", e, 0)).rearrange("p (k n) -> p k n", n=FE)
                    pe.wait_ge(s_xgTa, e + 1)
                    pe.wait_ge(s_xgTd, e + 1)
                    if e >= 2:
                        pe.wait_ge(s_hm, e - 1)
                    for j, w in enumerate((wg, wu)):
                        for k in range(KT):
                            last = mm(bank[e % 2][:, j * FE:(j + 1) * FE], xgT[e % 2][:, k, :],
                                      w[:, k, :], k == 0, k == KT - 1)
                    last.then_inc(s_in, 1)

                def turn_hidden(e):
                    pe.wait_ge(s_hm, e + 1)
                    if e >= 1:
                        pe.wait_ge(s_hte, e)
                    for k in range(FT):
                        last = turn(bank[6][:, k * P:(k + 1) * P], hg[e % 2][:, k * P:(k + 1) * P])
                    last.then_inc(s_ht, 1)

                def expert_out(e):
                    wd = weights(pe, ("wd", e, 0)).rearrange("p (k n) -> p k n", n=D)
                    pe.wait_ge(s_hte, e + 1)
                    if e >= 1:
                        pe.wait_ge(s_eoa, e)
                        pe.wait_ge(s_eod, e)
                    for c in range(2):
                        for k in range(FT):
                            last = mm(bank[4 + c][:], hT[e % 2][:, k * P:(k + 1) * P],
                                      wd[:, k, c * 512:(c + 1) * 512], k == 0, k == FT - 1)
                    last.then_inc(s_down, 1)

                for e in range(AHEAD):
                    slot_tokens(e)
                turn_input(0)
                for e in range(NE):
                    expert_in(e)
                    if e + AHEAD < NE:
                        slot_tokens(e + AHEAD)
                    if e:
                        expert_out(e - 1)
                    if e + 1 < NE:
                        turn_input(e + 1)
                    turn_hidden(e)
                expert_out(NE - 1)

        @block.scalar
        def _(act):
            def f(out, src, func, done, **kw):
                return nc.scalar.activation(out, src, func, **kw).then_inc(done, 1)

            act.dma_start(x[:, 0:TILES - 1, :], x_prompt[0].rearrange("(t p) d -> p t d", p=P))\
                .then_inc(s_x, 16)
            act.dma_start(x[0:NS, TILES - 1, :], x_sample.rearrange("b t d -> (b t) d"))\
                .then_inc(s_x, 16)
            act.dma_start(con[:], consts).then_inc(s_con, 16)

            act.wait_ge(s_c, 32)
            f(crow, crow, ACT.Silu, s_silu)
            act.wait_ge(s_zero, 4)
            act.wait_ge(s_x, 32)
            for t in range(TILES):
                n = rows(t)
                f(xn[0:n, t], x[0:n, t], ACT.Square, s_sq, accum_out=ss[0:n, 0, t, 0:1])
            act.wait_ge(s_sq, TILES)
            f(ss[:, 0, :, 0], ss[:, 0, :, 0], ACT.Sqrt, s_xrms, scale=1.0 / D, bias=eps[:, 0:1])
            act.wait_ge(s_spin, 1)
            f(softp[:, 1], softp[:, 0], ACT.Exp, s_spexp, scale=-1.0)
            act.wait_ge(s_spin, 2)
            f(softp[:, 3], softp[:, 2], ACT.Ln, s_spln)

            act.wait_ge(s_modT, 1)
            act.wait_ge(s_uTp, 7)
            for k in range(0, KT, 2):
                f(uT[:, k, 0:SEQ], bank[k % 7 + 1][:], ACT.Identity, s_uTa,
                  scale=modT[:, k % 4, 2 + k // 4, 0:1], bias=modT[:, k % 4, k // 4, 0:1])

            half = NTOK // 2

            def take_xr(m):
                b = xr[m % 2]
                smp = b[:, 3 + SEQ:].rearrange("p (b t) -> p b t", t=3 + DT)
                act.wait_ge(s_xr, m + 1)
                if m >= 2:
                    act.wait_ge(s_conv, m - 1)
                b0, b1 = bank[2 * (m % 2)], bank[2 * (m % 2) + 1]
                f(b[:, 3:3 + half], b0[:, 0:half], ACT.Copy, s_act)
                f(b[:, 3 + half:3 + SEQ], b1[:, 0:SEQ - half], ACT.Copy, s_act)
                f(smp[:, :, 3:], b1[:, SEQ - half:half].rearrange("p (b t) -> p b t", t=DT),
                  ACT.Copy, s_act)
                f(smp[:, :, 0:3], stT[:, m, 0:24].rearrange("p (b t) -> p b t", t=3),
                  ACT.Copy, s_xre)

            def sigmoids(m):
                act.wait_ge(s_gate, m + 1)
                if m >= 1:
                    act.wait_ge(s_lru, m)
                for gi, buf in ((0, R), (1, I)):
                    f(buf[:, 0:SEQ], bank[5 + gi][:], ACT.Sigmoid, s_act,
                      bias=parT[:, m, 5 + gi:6 + gi])
                    f(buf[:, SEQ:], bank[7][:, gi * NS:(gi + 1) * NS], ACT.Sigmoid, s_sig,
                      bias=parT[:, m, 5 + gi:6 + gi])
                act.wait_ge(s_sig, 2 * m + 2)
                if m == 0:
                    act.wait_ge(s_spout, 1)
                f(R, R, ACT.Tanh, s_tanh, scale=softp[:, 7, m:m + 1])
                act.wait_ge(s_tanh, m + 1)
                f(Z, R, ACT.Sqrt, s_root, scale=-1.0)

            def gelus(m):
                i = MT + m
                act.wait_ge(s_xr, i + 1)
                if m >= 1:
                    act.wait_ge(s_lru, MT)
                if m >= 2:
                    act.wait_ge(s_hy, m - 1)
                for n in range(2):
                    f(ge[m % 2][:, n * half:(n + 1) * half], bank[2 * (i % 2) + n][:, 0:half],
                      ACT.Gelu_apprx_tanh, s_act if n == 0 else s_yge)

            take_xr(0)
            take_xr(1)
            sigmoids(0)
            take_xr(2)
            sigmoids(1)
            take_xr(3)
            sigmoids(2)
            gelus(0)
            sigmoids(3)
            for m in range(1, MT):
                gelus(m)
            act.wait_ge(s_tailT, 1)
            f(tailrow[:], bank[7][0:36, :], ACT.Copy, s_tail)

            def take(t, c):
                n = rows(t)
                kind = NH * (t == TILES - 1)
                act.wait_ge(s_proj, 4 * t + c + 1)
                if c < 2:
                    dst, col = ((qs, C_DQ), (ks, C_DK))[c]
                    act.wait_ge(s_rot, 2 * t - 1 + c) if t else None
                    for h in range(NH):
                        f(dst[0:n, h * P:(h + 1) * P], bank[c][0:n, h * P:(h + 1) * P], ACT.Copy,
                          s_act if h < NH - 1 else s_pe,
                          scale=con[0:n, col + kind + h:col + kind + h + 1])
                elif c == 2:
                    if t >= 2:
                        act.wait_ge(s_kv, t - 1)
                    f(vv[t % 2][0:n], bank[c][0:n], ACT.Copy, s_pe)
                else:
                    if t >= 2:
                        act.wait_ge(s_ob, t - 1)
                    f(gg[t % 2][0:n], bank[c][0:n], ACT.Silu, s_pe)

            def take_qkT(t):
                n = rows(t)
                act.wait_ge(s_qkT, t + 1)
                if t:
                    act.wait_ge(s_o, t)
                for dst, b in ((qT, 4), (kT, 5)):
                    f(dst.rearrange("p (h i) -> p h i", i=P)[:, :, 0:n],
                      bank[b][:].rearrange("p (h i) -> p h i", i=P)[:, :, 0:n], ACT.Copy,
                      s_act if b == 4 else s_qkTe)

            def take_obT(t):
                n = rows(t)
                act.wait_ge(s_obT, t + 1)
                f(outbT[:, :, t * P:t * P + n],
                  bank[4][:].rearrange("p (h i) -> p h i", i=P)[:, :, 0:n], ACT.Copy, s_obTe)

            def deviation(t):
                n = rows(t)
                act.wait_ge(s_var, t + 1)
                f(grs[0:n], gmv[0:n, :, 1], ACT.Sqrt, s_dev, bias=eps[0:n, 1:2])

            act.wait_ge(s_modst, 16 * 8)
            for t in range(TILES + 1):
                for c in range(4):
                    if t < TILES:
                        take(t, c)
                    if t and c == 0:
                        take_qkT(t - 1)
                    if t == TILES and c == 2:
                        act.wait_ge(s_cross, NH)
                        f(sm[:, 0:NH * NS], bank[7][:, 0:NH * NS], ACT.Copy, s_oTe)
                    if t and c == 2:
                        deviation(t - 1)
                    if t and c == 3:
                        take_obT(t - 1)

            def square_m(t):
                n = rows(t)
                act.wait_ge(s_out, t + 1)
                for c in range(2):
                    f(junk[0:n, c * 512:(c + 1) * 512], bank[2 * (t % 2) + c][0:n], ACT.Square,
                      s_msq, accum_out=ss[0:n, 1, t, c:c + 1])
                act.wait_ge(s_msq, 2 * t + 2)
                f(ss[0:n, 1, t, 1:2], ss[0:n, 1, t, 1:2], ACT.Identity, s_msum, scale=1.0 / D,
                  bias=eps[0:n, 0:1])
                act.wait_ge(s_msum, t + 1)
                f(ss[0:n, 1, t, 0:1], ss[0:n, 1, t, 0:1], ACT.Sqrt, s_mrms, scale=1.0 / D,
                  bias=ss[0:n, 1, t, 1:2])

            def square_x(t):
                n = rows(t)
                act.wait_ge(s_x1, t + 1)
                f(junk[0:n], x[0:n, t], ACT.Square, s_xsq, accum_out=ss[0:n, 2, t, 0:1])
                act.wait_ge(s_xsq, t + 1)
                f(ss[0:n, 2, t, 0:1], ss[0:n, 2, t, 0:1], ACT.Sqrt, s_x1rms, scale=1.0 / D,
                  bias=eps[0:n, 0:1])

            def take_u2T(t):
                n = rows(t)
                for hf in range(2):
                    act.wait_ge(s_u2T, 2 * t + hf + 1)
                    f(uT[:, 4 * hf:4 * hf + 4, t * P:t * P + n],
                      bank[4 + hf][:].rearrange("p (k i) -> p k i", i=P)[:, :, 0:n], ACT.Copy,
                      s_u2Te)

            for t in range(TILES + 1):
                if t < TILES:
                    square_m(t)
                if t:
                    take_u2T(t - 1)
                if t < TILES:
                    square_x(t)
                    act.wait_ge(s_u2, t + 1)
                    act.dma_start(u2_dram[t * P:t * P + rows(t), :], u2[t % 2][0:rows(t)])\
                        .then_inc(s_u2st[t % 2], 16)

            act.wait_ge(s_gin, 1)
            f(gx[:, :, 0:NG], gx[:, :, 0:NG], ACT.Exp, s_gexp)
            act.wait_ge(s_gin, 2)
            f(gx[:, :, 4:5], gx[:, :, 4:5], ACT.Exp, s_gexp)

            for k in range(2):
                act.wait_ge(s_u2st[k], 16 * ((TILES + 1 - k) // 2))
            with act.If(overflow(act)):
                with act.Fori(0, NE) as e:
                    for t in range(TILES):
                        n = rows(t)
                        act.wait_ge(s_h1, e * TILES + t + 1)
                        f(hb[0][0:n], bank[0][0:n, 0:FE], ACT.Silu, s_h1e)
                        act.wait_ge(s_hTp, e * TILES + t + 2)
                        act.wait_ge(s_dn, e * TILES + t + 1)
                        f(hT[0].rearrange("p (k i) -> p k i", i=P)[:, :, 0:n],
                          bank[2][:, 0:FE].rearrange("p (k i) -> p k i", i=P)[:, :, 0:n],
                          ACT.Copy, s_hTe)
            with act.Else():
                def take_input(e):
                    act.wait_ge(s_xgT, e + 1)
                    if e >= 2:
                        act.wait_ge(s_in, e - 1)
                    f(xgT[e % 2][:, 0:4, :].rearrange("p k i -> p (k i)"), bank[2][:], ACT.Copy,
                      s_xgTa)

                def take_out(e):
                    act.wait_ge(s_down, e + 1)
                    if e >= 2:
                        act.wait_ge(s_ost[e % 2], 16 * (e // 2))
                    f(eo[e % 2][:, 0:512], bank[4][:], ACT.Copy, s_eoa)

                def store_out(e):
                    act.wait_ge(s_eoa, e + 1)
                    act.wait_ge(s_eod, e + 1)
                    act.dma_start(slots_dram[e * P:(e + 1) * P, :], eo[e % 2])\
                        .then_inc(s_ost[e % 2], 16)

                take_input(0)
                for e in range(NE):
                    act.wait_ge(s_in, e + 1)
                    if e >= 2:
                        act.wait_ge(s_hm, e - 1)
                    f(hb[e % 2], bank[e % 2][:, 0:FE], ACT.Silu, s_hs)
                    if e:
                        take_out(e - 1)
                    if e + 1 < NE:
                        take_input(e + 1)
                    act.wait_ge(s_ht, e + 1)
                    if e >= 2:
                        act.wait_ge(s_down, e - 1)
                    f(hT[e % 2], bank[6][:, 0:FE], ACT.Copy, s_hte)
                    if e:
                        store_out(e - 1)
                take_out(NE - 1)
                store_out(NE - 1)
            def store_y(t):
                act.wait_ge(s_fin, t + 1)
                dst = (y_prompt[0, t * P:(t + 1) * P, :] if t < TILES - 1
                       else y_sample.rearrange("b t d -> (b t) d"))
                act.dma_start(dst, x[0:rows(t), t, :]).then_inc(s_yout, 16)

            for t in range(TILES):
                n = rows(t)
                act.wait_ge(s_f, t + 1)
                if t:
                    act.wait_ge(s_fsq, t)
                f(yj[0:n], Y[0:n, t], ACT.Square, s_fsq, accum_out=ss[0:n, 3, t, 0:1])
                act.wait_ge(s_fsq, t + 1)
                f(ss[0:n, 3, t, 0:1], ss[0:n, 3, t, 0:1], ACT.Sqrt, s_frms, scale=1.0 / D,
                  bias=eps[0:n, 0:1])
                if t:
                    store_y(t - 1)
            store_y(TILES - 1)
            act.wait_ge(s_yout, 16 * TILES)

        @block.vector
        def _(dve):
            v = nc.vector
            count = [0]

            def link(ins):
                count[0] += 1
                ins.then_inc(s_vec, 1)
                dve.wait_ge(s_vec, count[0])

            dve.wait_ge(s_setupT, 1)
            v.tensor_copy(rowsT[:], bank[0][:, 0:416]).then_inc(s_rowsT, 1)
            dve.wait_ge(s_rowsT, 1)
            lam = parT[:, :, 7]
            v.scalar_tensor_tensor(out=softp[:, 0], in0=lam, scalar=-1.0, in1=lam, op0=ALU.mult,
                                   op1=ALU.max).then_inc(s_spin, 1)

            dve.wait_ge(s_xrms, 1)
            link(v.reciprocal(ss[:, 0, :, 0], ss[:, 0, :, 0]))
            for t in range(TILES):
                n = rows(t)
                v.tensor_scalar(xn[0:n, t], x[0:n, t], ss[0:n, 0, t, 0:1], None, ALU.mult)\
                    .then_inc(s_xn, 1)

            dve.wait_ge(s_spexp, 1)
            v.tensor_scalar(softp[:, 2], softp[:, 1], 1.0, None, ALU.add).then_inc(s_spin, 1)
            dve.wait_ge(s_spin, 2)
            link(v.tensor_scalar(softp[:, 4], softp[:, 2], -1.0, None, ALU.add))
            link(v.tensor_scalar(softp[:, 5], softp[:, 4], 0.0, None, ALU.is_equal))
            link(v.tensor_tensor(out=softp[:, 4], in0=softp[:, 4], in1=softp[:, 5], op=ALU.add))
            link(v.reciprocal(softp[:, 4], softp[:, 4]))
            dve.wait_ge(s_spln, 1)
            link(v.tensor_tensor(out=softp[:, 3], in0=softp[:, 3], in1=softp[:, 5], op=ALU.add))
            link(v.tensor_tensor(out=softp[:, 3], in0=softp[:, 3], in1=softp[:, 4], op=ALU.mult))
            link(v.tensor_tensor(out=softp[:, 3], in0=softp[:, 3], in1=softp[:, 1], op=ALU.mult))
            link(v.tensor_scalar(softp[:, 6], lam, -1.0, 0.0, ALU.mult, ALU.max))
            link(v.tensor_tensor(out=softp[:, 6], in0=softp[:, 6], in1=softp[:, 3], op=ALU.add))
            v.tensor_scalar(softp[:, 7], softp[:, 6], -4.0, None, ALU.mult).then_inc(s_spout, 1)

            def mod_rows(gq, b):
                if gq == 0:
                    dve.wait_ge(s_bm, 16 * 12)
                    dve.wait_ge(s_zero, 8)
                    link(v.tensor_scalar(bm[64:128, 0, :], bm[64:128, 0, :], 1.0, None, ALU.add))
                    link(v.tensor_scalar(bm[0:64, 2, :], bm[0:64, 2, :], 1.0, None, ALU.add))
                dve.wait_ge(s_mod, KT * (gq + 1))
                link(v.tensor_tensor(out=bm[:, gq], in0=bank[b][:], in1=bm[:, gq], op=ALU.add))
                v.tensor_tensor(out=bm[:, gq], in0=bm[:, gq], in1=nm[:, gq], op=ALU.mult)\
                    .then_inc(s_modrow, 1)

            mod_rows(0, 0)
            dve.wait_ge(s_modTp, 1)
            v.tensor_copy(modT[:].rearrange("p a b c -> p (a b c)"), bank[0][:]).then_inc(s_modT, 1)

            dve.wait_ge(s_modT, 1)
            for k in range(1, KT, 2):
                if k == 7:
                    dve.wait_ge(s_uTp, 8)
                v.tensor_scalar(uT[:, k, 0:SEQ], bank[k % 7 + 1][:],
                                modT[:, k % 4, 2 + k // 4, 0:1], modT[:, k % 4, k // 4, 0:1],
                                ALU.mult, ALU.add).then_inc(s_uTd, 1)
            dve.wait_ge(s_uTp, 9)
            for j in range(2):
                u = uT[:, 4 * j:4 * j + 4, SEQ:NTOK]
                for q in range(4):
                    row = lambda jj: modT[:, q, jj, 1:1 + DB].unsqueeze(2).to_broadcast([P, DB, DT])
                    uq = u[:, q].rearrange("p (b t) -> p b t", t=DT)
                    link(v.tensor_tensor(
                        out=uq, in0=bank[2][:, (4 * j + q) * NS:(4 * j + q + 1) * NS].rearrange(
                            "p (b t) -> p b t", t=DT), in1=row(2 + j), op=ALU.mult))
                    last = v.tensor_tensor(out=uq, in0=uq, in1=row(j), op=ALU.add)
                    link(last) if (j, q) != (1, 3) else last.then_inc(s_uTd, 1)

            def conv(m):
                b, o = xr[m % 2], xc[m % 2]
                smp = b[:, 3 + SEQ:].rearrange("p (b t) -> p b t", t=3 + DT)
                osm = o[:, SEQ:].rearrange("p (b t) -> p b t", t=DT)
                dve.wait_ge(s_xre, m + 1)
                if m >= 2:
                    dve.wait_ge(s_lru, m - 1)
                v.tensor_copy(tails[:, m, 0:3], b[:, SEQ:SEQ + 3]).then_inc(s_tl, 1)
                v.tensor_copy(tails[:, m, 3:27].rearrange("p (b t) -> p b t", t=3), smp[:, :, DT:])\
                    .then_inc(s_tl, 1)
                v.tensor_scalar(o[:, 0:SEQ], b[:, 0:SEQ], parT[:, m, 0:1], parT[:, m, 4:5],
                                ALU.mult, ALU.add)
                link(v.tensor_scalar(osm, smp[:, :, 0:DT], parT[:, m, 0:1], parT[:, m, 4:5],
                                     ALU.mult, ALU.add))
                for j in range(1, CONVW):
                    v.scalar_tensor_tensor(out=o[:, 0:SEQ], in0=b[:, j:j + SEQ],
                                           scalar=parT[:, m, j:j + 1], in1=o[:, 0:SEQ],
                                           op0=ALU.mult, op1=ALU.add)
                    last = v.scalar_tensor_tensor(out=osm, in0=smp[:, :, j:j + DT],
                                                  scalar=parT[:, m, j:j + 1], in1=osm,
                                                  op0=ALU.mult, op1=ALU.add)
                    link(last) if j < CONVW - 1 else last.then_inc(s_conv, 1)

            def rg_lru(m):
                dve.wait_ge(s_sig, 2 * m + 2)
                dve.wait_ge(s_conv, m + 1)
                link(v.tensor_tensor(out=I, in0=I, in1=xc[m % 2], op=ALU.mult))
                dve.wait_ge(s_tanh, m + 1)
                link(v.tensor_scalar(Q, R, -1.0, 1.0, ALU.mult, ALU.add))
                link(v.reciprocal(Q, Q))
                link(v.scalar_tensor_tensor(out=A, in0=R, scalar=1.0, in1=Q, op0=ALU.add,
                                            op1=ALU.mult))
                dve.wait_ge(s_root, m + 1)
                link(v.scalar_tensor_tensor(out=Q, in0=Z, scalar=2.0, in1=Q, op0=ALU.mult,
                                            op1=ALU.mult))
                link(v.tensor_tensor(out=I, in0=I, in1=Q, op=ALU.mult))
                A0 = A[:, SEQ:].rearrange("p (b t) -> p b t", t=DT)[:, :, 0]
                I0 = I[:, SEQ:].rearrange("p (b t) -> p b t", t=DT)[:, :, 0]
                link(v.tensor_tensor(out=Q[:, 0:DB], in0=A0, in1=stT[:, m, 24:32], op=ALU.mult))
                link(v.tensor_tensor(out=I0, in0=I0, in1=Q[:, 0:DB], op=ALU.add))
                link(v.tensor_scalar(A0, A0, 0.0, None, ALU.mult))
                v.tensor_tensor_scan(hy[:, m], A, I, 0.0, ALU.mult, ALU.add).then_inc(s_lru, 1)
                dve.wait_ge(s_lru, m + 1)
                v.tensor_copy(tails[:, m, 27:28], hy[:, m, SEQ - 1:SEQ]).then_inc(s_tl, 1)
                v.tensor_copy(tails[:, m, 28:36],
                              hy[:, m, SEQ:].rearrange("p (b t) -> p b t", t=DT)[:, :, DT - 1])\
                    .then_inc(s_h, 1)

            def gated(m):
                dve.wait_ge(s_yge, m + 1)
                dve.wait_ge(s_h, m + 1)
                v.tensor_tensor(out=hy[:, m], in0=hy[:, m], in1=ge[m % 2], op=ALU.mult)\
                    .then_inc(s_hy, 1)

            conv(0)
            conv(1)
            rg_lru(0)
            conv(2)
            rg_lru(1)
            conv(3)
            mod_rows(1, 4)
            rg_lru(2)
            gated(0)
            rg_lru(3)
            for m in range(1, MT):
                gated(m)
            mod_rows(2, 4)

            def rotate(t, c):
                n = rows(t)
                src, dst = ((qs, qr), (ks, kr[t % 2]))[c]
                halves = lambda r: r[0:n].rearrange("p (h z d) -> p h z d", z=2, d=64)
                cs = cosv[0:n, t][:, None, :].to_broadcast([n, 2 * NH, 64])
                sn = sinv[0:n, t][:, None, :].to_broadcast([n, NH, 64])
                dve.wait_ge(s_pe, 4 * t + c + 1)
                if t or c:
                    dve.wait_ge(s_rot, 2 * t + c)
                if c == 0 and t:
                    dve.wait_ge(s_qkT, t)
                if c == 1 and t >= 2:
                    dve.wait_ge(s_kv, t - 1)
                v.tensor_tensor(out=dst[0:n].rearrange("p (h d) -> p h d", d=64),
                                in0=src[0:n].rearrange("p (h d) -> p h d", d=64), in1=cs,
                                op=ALU.mult)
                v.tensor_tensor(out=halves(tB)[:, :, 0], in0=halves(src)[:, :, 1], in1=sn,
                                op=ALU.mult)
                link(v.tensor_tensor(out=halves(tB)[:, :, 1], in0=halves(src)[:, :, 0], in1=sn,
                                     op=ALU.mult))
                link(v.tensor_tensor(out=halves(dst)[:, :, 0], in0=halves(dst)[:, :, 0],
                                     in1=halves(tB)[:, :, 0], op=ALU.subtract))
                v.tensor_tensor(out=halves(dst)[:, :, 1], in0=halves(dst)[:, :, 1],
                                in1=halves(tB)[:, :, 1], op=ALU.add).then_inc(s_rot, 1)

            def mask(t):
                n = rows(t)
                m0 = C_MP if t < TILES - 1 else C_MS
                dve.wait_ge(s_sc, t + 1)
                if t:
                    dve.wait_ge(s_o, t)
                v.tensor_tensor(out=sm[0:n, 0:NH * n].rearrange("p (h i) -> p h i", i=n),
                                in0=bank[6][0:n, 0:NH * n].rearrange("p (h i) -> p h i", i=n),
                                in1=con[0:n, m0:m0 + n][:, None, :].to_broadcast([n, NH, n]),
                                op=ALU.mult).then_inc(s_sm, 1)

            def advance(t):
                dve.wait_ge(s_kv, t + 1)
                dve.wait_ge(s_o, t + 1)
                if t == 0:
                    src = bank[5]
                else:
                    link(v.tensor_tensor(out=tS, in0=S, in1=bank[5][:], op=ALU.add))
                    src = tS
                for h in range(NH):
                    c = slice(h * P, (h + 1) * P)
                    last = v.tensor_scalar(S[:, c], src[:, c], GAMMA_CHUNK[h], None, ALU.mult)
                last.then_inc(s_st, 1)

            def group_norm(t):
                n = rows(t)
                o = bank[7 if t < TILES - 1 else 6]
                dve.wait_ge(s_o, t + 1)
                if t:
                    dve.wait_ge(s_obT, t)
                for h in range(NH):
                    last = v.bn_stats(gst[0:n, h], o[0:n, h * P:(h + 1) * P])
                link(last)
                for h in range(NH):
                    last = v.bn_aggr(gmv[0:n, h], gst[0:n, h])
                last.then_inc(s_var, 1)
                dve.wait_ge(s_dev, t + 1)
                link(v.reciprocal(grs[0:n], grs[0:n]))
                for h in range(NH):
                    c = slice(h * P, (h + 1) * P)
                    last = v.tensor_scalar(ob[0:n, c], o[0:n, c], gmv[0:n, h, 0:1],
                                           grs[0:n, h:h + 1], ALU.subtract, ALU.mult)
                link(last)
                dve.wait_ge(s_gg, t + 1)
                v.tensor_tensor(out=ob[0:n], in0=ob[0:n], in1=gg[t % 2][0:n], op=ALU.mult)\
                    .then_inc(s_ob, 1)

            def gate_weight(t):
                n = rows(t)
                dve.wait_ge(s_pe, 4 * t + 4)
                dve.wait_ge(s_misc, 16 * 5)
                v.tensor_tensor(out=gg[t % 2][0:n], in0=gg[t % 2][0:n], in1=gnw[0:n], op=ALU.mult)\
                    .then_inc(s_gg, 1)

            def sample_states():
                for h in range(NH):
                    dve.wait_ge(s_cross, h + 1)
                    for n in range(2):
                        part = s0[h % 2][:, 4 * n:4 * n + 4, :].rearrange("p b e -> p (b e)")
                        dve.wait_ge(s_skv, 2 * h + n + 1)
                        link(v.tensor_tensor(out=part, in0=part, in1=bank[4 + n][:], op=ALU.add))
                        v.tensor_scalar(part, part, GAMMA_STEP[h], None, ALU.mult)\
                            .then_inc(s_snew, 1)

            for t in range(TILES + 1):
                if t < TILES:
                    rotate(t, 0)
                if t:
                    mask(t - 1)
                if t < TILES:
                    rotate(t, 1)
                if t == TILES:
                    sample_states()
                elif t:
                    advance(t - 1)
                if t:
                    group_norm(t - 1)
                if t < TILES:
                    gate_weight(t)

            tag = lambda t: "p" if t < TILES - 1 else "s"

            def after_mixer(t):
                n = rows(t)
                dve.wait_ge(s_mrms, t + 1)
                link(v.reciprocal(ss[0:n, 1, t, 0:1], ss[0:n, 1, t, 0:1]))
                if t == 0:
                    dve.wait_ge(s_tab, 16 * 27)
                    dve.wait_ge(s_ssto, 16 * NH)
                for c in range(2):
                    w = slice(c * 512, (c + 1) * 512)
                    last = v.scalar_tensor_tensor(
                        out=t1[0:n, w], in0=bank[2 * (t % 2) + c][0:n],
                        scalar=ss[0:n, 1, t, 0:1], in1=tab["g1" + tag(t)][0:n, w], op0=ALU.mult,
                        op1=ALU.mult)
                link(last)
                v.tensor_tensor(out=x[0:n, t], in0=x[0:n, t], in1=t1[0:n], op=ALU.add)\
                    .then_inc(s_x1, 1)
                dve.wait_ge(s_x1rms, t + 1)
                link(v.reciprocal(ss[0:n, 2, t, 0:1], ss[0:n, 2, t, 0:1]))
                if t >= 2:
                    dve.wait_ge(s_u2T, 2 * (t - 1))
                    dve.wait_ge(s_u2st[t % 2], 16 * (t // 2))
                link(v.scalar_tensor_tensor(
                    out=u2[t % 2][0:n], in0=x[0:n, t], scalar=ss[0:n, 2, t, 0:1],
                    in1=tab["a2" + tag(t)][0:n], op0=ALU.mult, op1=ALU.mult))
                v.tensor_tensor(out=u2[t % 2][0:n], in0=u2[t % 2][0:n],
                                in1=tab["s2" + tag(t)][0:n], op=ALU.add).then_inc(s_u2, 1)

            def take_logits(t):
                n = rows(t)
                dve.wait_ge(s_rtr, t + 1)
                v.tensor_tensor(out=logit[0:n, t], in0=bank[6][0:n, 0:NG + NE], in1=brt[0:n],
                                op=ALU.add).then_inc(s_lg, 1)

            v.tensor_copy(tri[:], con[:, C_TRI:C_TRI + P]).then_inc(s_half, 1)
            v.memset(ones[:], 1.0).then_inc(s_half, 1)
            v.tensor_copy(tok[:], con[:, C_TOK:C_TOK + TILES]).then_inc(s_half, 1)
            v.memset(logit[:], 0.0).then_inc(s_tl, 1)
            dve.wait_ge(s_tl, 3 * MT + 1)
            for t in range(TILES + 1):
                if t < TILES:
                    after_mixer(t)
                if t:
                    take_logits(t - 1)

            dve.wait_ge(s_lg, TILES)
            T5 = [P, TILES, NG]
            lg, le = logit[:, :, 0:NG], logit[:, :, NG:]
            rev = con[:, C_REV:C_REV + NG][:, None, :].to_broadcast(T5)

            def tt(out, a, b, op):
                link(v.tensor_tensor(out=out, in0=a, in1=b, op=op))

            def first_max(src, top, onehot):
                link(v.tensor_reduce(out=top, in_=src, axis=AX.X, op=ALU.max))
                tt(onehot, src, top.unsqueeze(2).to_broadcast(T5), ALU.is_equal)
                tt(onehot, onehot, rev, ALU.mult)
                link(v.tensor_reduce(out=rtmp, in_=onehot, axis=AX.X, op=ALU.max))
                tt(onehot, onehot, rtmp.unsqueeze(2).to_broadcast(T5), ALU.is_equal)

            first_max(lg, rtop, rgrp)
            tt(rgrp, rgrp, con[:, C_VALID:C_VALID + TILES].unsqueeze(2).to_broadcast(T5), ALU.mult)
            v.tensor_tensor(out=gx[:, :, 0:NG], in0=lg, in1=rtop.unsqueeze(2).to_broadcast(T5),
                            op=ALU.subtract).then_inc(s_gin, 1)
            for e in range(EPG):
                tt(rsel, le.rearrange("p t (g e) -> p t g e", e=EPG)[:, :, :, e], rgrp, ALU.mult)
                link(v.tensor_reduce(out=rin[:, :, e], in_=rsel, axis=AX.X, op=ALU.add))
            first_max(rin, rm1, roh1)
            link(v.tensor_scalar(rsel, roh1, -3.0e38, None, ALU.mult))
            link(v.tensor_scalar(rin2, roh1, -1.0, 1.0, ALU.mult, ALU.add))
            tt(rin2, rin2, rin, ALU.mult)
            tt(rin2, rin2, rsel, ALU.add)
            first_max(rin2, rm2, roh2)
            v.tensor_tensor(out=gx[:, :, 4], in0=rm2, in1=rm1, op=ALU.subtract).then_inc(s_gin, 1)
            for k, r in enumerate((roh1, roh2)):
                link(v.tensor_tensor(
                    out=oh[k].rearrange("p t (g e) -> p t g e", e=EPG),
                    in0=r[:, :, None, :].to_broadcast([P, TILES, NG, EPG]),
                    in1=rgrp.unsqueeze(3).to_broadcast([P, TILES, NG, EPG]), op=ALU.mult))
            v.tensor_tensor(out=sel[:], in0=oh[0], in1=oh[1], op=ALU.add).then_inc(s_rsel, 1)
            dve.wait_ge(s_gexp, 2)
            link(v.tensor_reduce(out=rtop, in_=gx[:, :, 0:NG], axis=AX.X, op=ALU.add))
            link(v.tensor_scalar(rtmp, gx[:, :, 4], 1.0, None, ALU.add))
            tt(rtmp, rtmp, rtop, ALU.mult)
            link(v.reciprocal(rm1, rtmp))
            tt(rm2, gx[:, :, 4], rm1, ALU.mult)

            dve.wait_ge(s_rank, 1)
            link(v.tensor_reduce(out=count1, in_=bank[7][:, TILES * NE:(TILES + 1) * NE], axis=AX.X,
                                 op=ALU.max))
            v.tensor_scalar(over[:], count1, float(CAPACITY), None, ALU.is_gt).then_inc(s_over, 1)

            for k in range(2):
                dve.wait_ge(s_u2st[k], 16 * ((TILES + 1 - k) // 2))
            with dve.If(overflow(dve)):
                gv = lambda r: r.rearrange("p t (g e) -> p (t g) e", e=EPG)
                w16 = lambda w: w.unsqueeze(2).to_broadcast([P, TILES, NE])
                v.tensor_tensor(out=oh[0], in0=oh[0], in1=w16(rm1), op=ALU.mult).then_inc(s_fb, 1)
                v.tensor_tensor(out=oh[1], in0=oh[1], in1=w16(rm2), op=ALU.mult).then_inc(s_fb, 1)
                dve.wait_ge(s_fb, 2)
                v.tensor_tensor(out=gates[:], in0=oh[0], in1=oh[1], op=ALU.add).then_inc(s_fb, 1)
                v.memset(Y.rearrange("p t d -> p (t d)"), 0.0).then_inc(s_fb, 1)
                dve.wait_ge(s_fb, 4)
                for s in (s_h2, s_hTp, s_dn, s_y):
                    dve.engine_nop().then_inc(s, 1)
                with dve.Fori(0, NE) as e:
                    dve.wait_ge(s_h2, e * TILES + 1)
                    v.tensor_copy(gcol, gates[:, :, bass.ds(e, 1)]).then_inc(s_gcol, 1)
                    dve.wait_ge(s_gcol, e + 1)
                    for t in range(TILES):
                        n = rows(t)
                        dve.wait_ge(s_h1e, e * TILES + t + 1)
                        dve.wait_ge(s_hTp, e * TILES + t + 1)
                        v.scalar_tensor_tensor(out=hg[0][0:n], in0=hb[0][0:n],
                                               scalar=gcol[0:n, t, 0:1],
                                               in1=bank[0][0:n, FE:2 * FE], op0=ALU.mult,
                                               op1=ALU.mult).then_inc(s_h2, 1)
                        dve.wait_ge(s_dn, e * TILES + t + 2)
                        dve.wait_ge(s_y, e * TILES + 1)
                        for c in range(2):
                            o = Y[0:n, t, c * 512:(c + 1) * 512]
                            last = v.tensor_tensor(out=o, in0=o, in1=bank[4 + c][0:n], op=ALU.add)
                        last.then_inc(s_y, 1)
                dve.wait_ge(s_y, NE * TILES + 1)
                dve.engine_nop().then_inc(s_f, TILES)
            with dve.Else():
                steps = [0]

                def then(ins):
                    steps[0] += 1
                    ins.then_inc(s_sp, 1)
                    dve.wait_ge(s_sp, steps[0])

                ranks = bank[7][:, 0:TILES * NE].rearrange("p (t e) -> p t e", e=NE)
                then(v.scalar_tensor_tensor(out=rank1.rearrange("p t e -> p (t e)"),
                                            in0=bank[7][:, 0:TILES * NE], scalar=1.0,
                                            in1=sel[:].rearrange("p t e -> p (t e)"), op0=ALU.add,
                                            op1=ALU.mult))
                v.tensor_tensor(out=place, in0=ranks, in1=con[:, None, C_BASE:C_BASE + NE]
                                .to_broadcast([P, TILES, NE]), op=ALU.add).then_inc(s_hit0, 1)
                dve.wait_ge(s_hit0, 1)

                def hits(e):
                    if e >= 2:
                        dve.wait_ge(s_tokn, e - 1)
                    shape = [P, TILES, P]
                    v.tensor_tensor(out=hit[e % 2],
                                    in0=con[:, None, C_IOTA:C_IOTA + P].to_broadcast(shape),
                                    in1=rank1[:, :, e:e + 1].to_broadcast(shape),
                                    op=ALU.is_equal).then_inc(s_hit, 1)

                def numbers(e):
                    dve.wait_ge(s_tokn, e + 1)
                    v.tensor_copy(slot_tok[:, e:e + 1], bank[7][:, 128:129]).then_inc(s_idx, 1)

                def take_input(e):
                    dve.wait_ge(s_xgT, e + 1)
                    if e >= 2:
                        dve.wait_ge(s_in, e - 1)
                    v.tensor_copy(xgT[e % 2][:, 4:8, :].rearrange("p k i -> p (k i)"), bank[3][:])\
                        .then_inc(s_xgTd, 1)

                def take_out(e):
                    dve.wait_ge(s_down, e + 1)
                    if e >= 2:
                        dve.wait_ge(s_ost[e % 2], 16 * (e // 2))
                    v.tensor_copy(eo[e % 2][:, 512:1024], bank[5][:]).then_inc(s_eod, 1)

                for e in range(AHEAD):
                    hits(e)
                    numbers(e)
                for k in range(2):
                    then(v.tensor_tensor(out=oh[k], in0=oh[k], in1=place, op=ALU.mult))
                    then(v.tensor_reduce(out=slotf, in_=oh[k], axis=AX.X, op=ALU.add))
                    last = v.tensor_copy(tok_slot[:, k], slotf)
                    then(last) if k == 0 else last.then_inc(s_place, 1)
                take_input(0)
                for e in range(NE):
                    if e + AHEAD < NE:
                        hits(e + AHEAD)
                    dve.wait_ge(s_hs, e + 1)
                    if e >= 2:
                        dve.wait_ge(s_ht, e - 1)
                    v.tensor_tensor(out=hg[e % 2], in0=hb[e % 2], in1=bank[e % 2][:, FE:2 * FE],
                                    op=ALU.mult).then_inc(s_hm, 1)
                    if e + AHEAD < NE:
                        numbers(e + AHEAD)
                    if e:
                        take_out(e - 1)
                    if e + 1 < NE:
                        take_input(e + 1)
                take_out(NE - 1)
                for t in range(TILES):
                    n = rows(t)
                    dve.wait_ge(s_og[t % 2], 32 * (t // 2 + 1))
                    then(v.tensor_scalar(Y[0:n, t], og[t % 2][0][0:n], rm1[0:n, t:t + 1], None,
                                         ALU.mult))
                    v.scalar_tensor_tensor(out=Y[0:n, t], in0=og[t % 2][1][0:n],
                                           scalar=rm2[0:n, t:t + 1], in1=Y[0:n, t], op0=ALU.mult,
                                           op1=ALU.add).then_inc(s_f, 1)
            for t in range(TILES):
                n = rows(t)
                dve.wait_ge(s_frms, t + 1)
                link(v.reciprocal(ss[0:n, 3, t, 0:1], ss[0:n, 3, t, 0:1]))
                if t == 0:
                    dve.wait_ge(s_g2, 16 * 9)
                link(v.scalar_tensor_tensor(
                    out=Y[0:n, t], in0=Y[0:n, t], scalar=ss[0:n, 3, t, 0:1],
                    in1=tab["g2" + tag(t)][0:n], op0=ALU.mult, op1=ALU.mult))
                v.tensor_tensor(out=x[0:n, t], in0=x[0:n, t], in1=Y[0:n, t], op=ALU.add)\
                    .then_inc(s_fin, 1)


_INS = ['x_prompt', 'x_sample', 'state_conv', 'state_lru', 'state_ret', 'c_prompt', 'c_sample',
        'w_mod', 'b_mod', 'norm_pre_mix', 'norm_post_mix', 'norm_pre_ffn', 'norm_post_ffn', 'w_in',
        'conv_w', 'conv_b', 'w_rgate', 'b_rgate', 'w_igate', 'b_igate', 'lru_lambda', 'ret_gn_w',
        'w_out', 'w_router_group', 'b_router_group', 'w_router_expert', 'b_router_expert',
        'w_exp_gate', 'w_exp_up', 'w_exp_down']
_OUTS = [(1, SEQ, D), (DB, DT, D), (1, 1, CONVW - 1, DL), (1, 1, DL), (1, 1, NH, DK, DK),
         (1, DB, CONVW - 1, DL), (1, DB, DL), (1, DB, NH, DK, DK)]


def kernel(**inputs):
    import concourse.bacc as _bacc
    from concourse.bass_utils import run_bass_kernel_spmd as _run

    nc = _bacc.Bacc("TRN2", target_bir_lowering=False, num_devices=1)
    arrays, args = {}, []
    for name in _INS:
        a = np.ascontiguousarray(inputs[name])
        arrays[f"in_{name}_dram"] = a
        args.append(nc.dram_tensor(f"in_{name}_dram", a.shape, F32, kind="ExternalInput").ap())
    arrays["in_consts_dram"] = shape_constants()
    args.append(nc.dram_tensor("in_consts_dram", (P, NCONST), F32, kind="ExternalInput").ap())
    for i, shape in enumerate(_OUTS):
        args.append(nc.dram_tensor(f"out_{i}_dram", shape, F32, kind="ExternalOutput").ap())
    build(nc, *args)
    r = _run(nc, [arrays], core_ids=[0])
    return tuple(r.results[0][f"out_{i}_dram"] for i in range(len(_OUTS)))
```
